# Optimizing a Trainium2 kernel written in Bass

```python
import jax, jax.numpy as jnp
from jax import lax
import numpy as np

D_MODEL = 2048
BATCH = 1
SEQ = 256
DEPTH = 1

RET_HEADS = 8
RET_DK = 128
RET_DV = 256
RET_CHUNK = 128
ROPE_BASE = 10000.0
SWA_Q_HEADS = 16
SWA_KV_HEADS = 4
SWA_HEAD_DIM = 64
SWA_WINDOW = 128
SWA_BLOCK = 128
D_FF = 5632
CONV_WIDTH = 3
RMS_EPS = 1e-6

RET_QK_W = RET_HEADS * RET_DK
RET_V_W = RET_HEADS * RET_DV
SWA_Q_W = SWA_Q_HEADS * SWA_HEAD_DIM
SWA_KV_W = SWA_KV_HEADS * SWA_HEAD_DIM
IN_WIDTHS = (RET_QK_W, RET_QK_W, RET_V_W, RET_V_W, SWA_Q_W, SWA_KV_W, SWA_KV_W, D_MODEL, D_MODEL)
IN_WIDTH = sum(IN_WIDTHS)
IN_SPLITS = tuple(int(s) for s in np.cumsum(IN_WIDTHS)[:-1])

kernel_name = "hybrid_retention_swa_sink_convffn"

def rmsnorm(x, g):
    xf = x.astype(jnp.float32)
    y = xf * lax.rsqrt(jnp.mean(xf * xf, axis=-1, keepdims=True) + RMS_EPS)
    return (y * g.astype(jnp.float32)).astype(x.dtype)

def rotary(x, pos):
    d = x.shape[-1]
    inv = 1.0 / (ROPE_BASE ** (jnp.arange(0, d, 2, dtype=jnp.float32) / d))
    ang = pos.astype(jnp.float32)[:, None] * inv[None, :]
    cos = jnp.cos(ang)[None, :, None, :]
    sin = jnp.sin(ang)[None, :, None, :]
    x1, x2 = x[..., : d // 2], x[..., d // 2:]
    return jnp.concatenate([x1 * cos - x2 * sin, x1 * sin + x2 * cos], axis=-1)

def retention_chunkwise(q, k, v):
    B, S, H, dk = q.shape
    dv = v.shape[-1]
    C = RET_CHUNK
    N = S // C
    log_gamma = jnp.log(1.0 - 2.0 ** (-5.0 - jnp.arange(H, dtype=jnp.float32)))
    idx = jnp.arange(C, dtype=jnp.float32)
    rel = idx[:, None] - idx[None, :]
    inner_decay = jnp.where(rel[None] >= 0,
                            jnp.exp(log_gamma[:, None, None] * jnp.maximum(rel, 0.0)[None]), 0.0)
    xi = jnp.exp(log_gamma[:, None] * (idx + 1.0))[None, :, :, None]
    zeta = jnp.exp(log_gamma[:, None] * (C - 1.0 - idx))[None, :, :, None]
    chunk_decay = jnp.exp(log_gamma * C)[None, :, None, None]
    k = k * (dk ** -0.5)

    def to_chunks(t):
        return t.reshape(B, N, C, H, t.shape[-1]).transpose(1, 0, 3, 2, 4)

    def step(state, inp):
        qi, ki, vi = inp
        scores = jnp.einsum('bhqd,bhkd->bhqk', qi, ki) * inner_decay[None]
        inner = jnp.einsum('bhqk,bhkv->bhqv', scores, vi)
        cross = jnp.einsum('bhqd,bhdv->bhqv', qi, state) * xi
        new_state = state * chunk_decay + jnp.einsum('bhkd,bhkv->bhdv', ki * zeta, vi)
        return new_state, inner + cross

    init = jnp.zeros((B, H, dk, dv), jnp.float32)
    _, out = lax.scan(step, init, (to_chunks(q), to_chunks(k), to_chunks(v)))
    return out.transpose(1, 0, 3, 2, 4).reshape(B, S, H, dv)

def swa_attention_sinks(q, k, v, sinks):
    B, S, Hq, dh = q.shape
    Hkv = k.shape[2]
    G = Hq // Hkv
    C = SWA_BLOCK
    N = S // C
    qb = q.astype(jnp.float32).reshape(B, N, C, Hkv, G, dh)

    def with_prev(t):
        tb = t.astype(jnp.float32).reshape(B, N, C, Hkv, dh)
        prev = jnp.pad(tb[:, :-1], ((0, 0), (1, 0), (0, 0), (0, 0), (0, 0)))
        return jnp.concatenate([prev, tb], axis=2)

    kw = with_prev(k)
    vw = with_prev(v)
    scores = jnp.einsum('bnqhgd,bnkhd->bnhgqk', qb, kw) * (dh ** -0.5)
    qpos = jnp.arange(C)[:, None] + C
    kpos = jnp.arange(2 * C)[None, :]
    relp = qpos - kpos
    band = (relp >= 0) & (relp < SWA_WINDOW)
    blk = jnp.arange(N)
    valid = band[None] & ((blk[:, None, None] > 0) | (kpos[None] >= C))
    scores = jnp.where(valid[None, :, None, None], scores, -jnp.inf)
    sink = sinks.astype(jnp.float32).reshape(Hkv, G)[None, None, :, :, None, None]
    m = jnp.maximum(jnp.max(scores, axis=-1, keepdims=True), sink)
    e = jnp.exp(scores - m)
    p = e / (jnp.sum(e, axis=-1, keepdims=True) + jnp.exp(sink - m))
    out = jnp.einsum('bnhgqk,bnkhd->bnqhgd', p, vw)
    return out.reshape(B, S, Hq * dh)

def causal_depthwise_conv(u, w, b):
    S = u.shape[1]
    up = jnp.pad(u, ((0, 0), (CONV_WIDTH - 1, 0), (0, 0)))
    y = b
    for kk in range(CONV_WIDTH):
        y = y + up[:, kk:kk + S] * w[kk]
    return y

def setup_inputs(seed: int = 0) -> dict:
    key = jax.random.key(seed)
    ks = jax.random.split(key, 16)
    f = jnp.float32
    L = DEPTH

    def nrm(k, shape, scale):
        return jax.random.normal(k, shape, f) * scale

    return {
        "x": jax.random.normal(ks[0], (BATCH, SEQ, D_MODEL), f),
        "g_pre_mix": 1.0 + nrm(ks[1], (L, D_MODEL), 0.02),
        "w_in": nrm(ks[2], (L, D_MODEL, IN_WIDTH), D_MODEL ** -0.5),
        "w_ret_o": nrm(ks[3], (L, RET_V_W, D_MODEL), RET_V_W ** -0.5),
        "w_swa_o": nrm(ks[4], (L, SWA_Q_W, D_MODEL), SWA_Q_W ** -0.5),
        "w_out": nrm(ks[5], (L, D_MODEL, D_MODEL), D_MODEL ** -0.5),
        "swa_sinks": nrm(ks[6], (L, SWA_Q_HEADS), 0.5),
        "g_post_mix": 1.0 + nrm(ks[7], (L, D_MODEL), 0.02),
        "g_pre_ffn": 1.0 + nrm(ks[8], (L, D_MODEL), 0.02),
        "w_up": nrm(ks[9], (L, D_MODEL, 2 * D_FF), D_MODEL ** -0.5),
        "conv_w": nrm(ks[10], (L, CONV_WIDTH, 2 * D_FF), CONV_WIDTH ** -0.5),
        "conv_b": nrm(ks[11], (L, 2 * D_FF), 0.01),
        "w_down": nrm(ks[12], (L, D_FF, D_MODEL), D_FF ** -0.5),
        "g_post_ffn": 1.0 + nrm(ks[13], (L, D_MODEL), 0.02),
    }

def reference(x, g_pre_mix, w_in, w_ret_o, w_swa_o, w_out, swa_sinks, g_post_mix,
              g_pre_ffn, w_up, conv_w, conv_b, w_down, g_post_ffn):
    B, S, _ = x.shape
    pos = jnp.arange(S, dtype=jnp.int32)
    for l in range(DEPTH):
        h = rmsnorm(x, g_pre_mix[l])
        proj = h @ w_in[l]
        rq, rk, rv, rg, sq, sk, sv, gr, gs = jnp.split(proj, IN_SPLITS, axis=-1)

        rq = rotary(rq.astype(jnp.float32).reshape(B, S, RET_HEADS, RET_DK), pos)
        rk = rotary(rk.astype(jnp.float32).reshape(B, S, RET_HEADS, RET_DK), pos)
        rv = rv.astype(jnp.float32).reshape(B, S, RET_HEADS, RET_DV)
        ret = retention_chunkwise(rq, rk, rv)
        ret = ret * lax.rsqrt(jnp.mean(ret * ret, axis=-1, keepdims=True) + RMS_EPS)
        ret = (jax.nn.silu(rg.astype(jnp.float32)) * ret.reshape(B, S, RET_V_W)).astype(x.dtype)
        ret_out = ret @ w_ret_o[l]

        swa = swa_attention_sinks(sq.reshape(B, S, SWA_Q_HEADS, SWA_HEAD_DIM),
                                  sk.reshape(B, S, SWA_KV_HEADS, SWA_HEAD_DIM),
                                  sv.reshape(B, S, SWA_KV_HEADS, SWA_HEAD_DIM),
                                  swa_sinks[l]).astype(x.dtype)
        swa_out = swa @ w_swa_o[l]

        mixed = jax.nn.sigmoid(gr) * ret_out + jax.nn.sigmoid(gs) * swa_out
        x = x + rmsnorm(mixed @ w_out[l], g_post_mix[l])

        h = rmsnorm(x, g_pre_ffn[l])
        u = causal_depthwise_conv(h @ w_up[l], conv_w[l], conv_b[l])
        val, gate = jnp.split(u, 2, axis=-1)
        y = (jax.nn.gelu(gate, approximate=True) * val) @ w_down[l]
        x = x + rmsnorm(y, g_post_ffn[l])
    return x


_drawn_inputs = setup_inputs


def setup_inputs(seed=0):
    import zlib

    import numpy as np

    out = dict(_drawn_inputs(seed))
    spreads = {}
    factors = {'swa_sinks': 5.094,
     'g_post_mix': 3.433,
     'g_pre_ffn': 3.452,
     'conv_b': 6.883,
     'g_post_ffn': 4.806}
    for name, (base, spread) in spreads.items():
        noise = np.random.default_rng([zlib.crc32(name.encode()), seed]).standard_normal(out[name].shape)
        drawn = base * np.exp(spread * noise) if base else spread * noise
        out[name] = __import__('jax').numpy.asarray(drawn.astype(out[name].dtype))
    for name, factor in factors.items():
        out[name] = (out[name] * factor).astype(out[name].dtype)
    return out
```

```python
from contextlib import ExitStack

import numpy as np

import concourse.bass as bass
from concourse import mybir

ALU = mybir.AluOpType
ACT = mybir.ActivationFunctionType
AX = mybir.AxisListType
F32 = mybir.dt.float32
F32R = mybir.dt.float32r
I32 = mybir.dt.int32

P = 128
D_MODEL = 2048
SEQ = 256
TT = SEQ // P
KT = D_MODEL // P
RET_HEADS, RET_DK, RET_DV = 8, 128, 256
SWA_HEADS, SWA_KV, SWA_DH, WINDOW = 16, 4, 64, 128
D_FF = 5632
EPS = 1e-6
NB = 512
CHUNK = 2048
HALF = CHUNK // 2
RAW_SLOTS = 4
HALF_SLOTS = 4

SK_AT = 0
SV_AT = SK_AT + SWA_KV * SWA_DH
RQ_AT = SV_AT + SWA_KV * SWA_DH
RK_AT = RQ_AT + RET_HEADS * RET_DK
RV_AT = RK_AT + RET_HEADS * RET_DK
SQ_AT = RV_AT + RET_HEADS * RET_DV
RG_AT = SQ_AT + SWA_HEADS * SWA_DH
GR_AT = RG_AT + RET_HEADS * RET_DV
GS_AT = GR_AT + D_MODEL
PROJ_W = GS_AT + D_MODEL
PROJ_BLOCKS = PROJ_W // NB

G_MERGE = PROJ_BLOCKS
G_OUT = G_MERGE + 6
G_UP = G_OUT + 4
UP_GROUPS = D_FF // 256
G_DOWN = G_UP + UP_GROUPS
DOWN_GROUPS = D_FF // (4 * P)
GROUPS = G_DOWN + DOWN_GROUPS
H_MERGE, H_OUT, H_UP, H_DOWN = (8 * g for g in (G_MERGE, G_OUT, G_UP, G_DOWN))
FF_TILES = D_FF // P

FILL_H = 0
FILL_SWA = FILL_H + KT // 2
FILL_RET = FILL_SWA + 4
FILL_MIX = FILL_RET + KT // 2
FILL_H2 = FILL_MIX + KT // 2

MASKED = -3.0e38
RSQRT_MAGIC = float(0x5F3759DF)


def fill_bank(f):
    return 4 + f % 4


def build(nc, weights, x, g_pre, g_ffn, g_post_mix, g_post_ffn, sinks, conv, ident, decay, rope, band, out):
    with ExitStack() as ctx:
        base = (nc.sbuf_base + 31) // 32 * 32

        def place(name, shape, dt, at):
            return nc.alloc_sbuf_tensor_at(name, shape, dt, offset=base + at)

        def sem(name):
            return ctx.enter_context(nc.semaphore(name))

        RAW_AT = 0
        HI_AT = RAW_AT + RAW_SLOTS * CHUNK * 4
        LO_AT = HI_AT + HALF_SLOTS * HALF * 4
        XT_AT = LO_AT + HALF_SLOTS * HALF * 4
        NAT0_AT = XT_AT + KT * 2 * SEQ * 4
        NAT1_AT = NAT0_AT + PROJ_W * 4
        X_AT = NAT1_AT + PROJ_W * 4
        SMALL_AT = X_AT + TT * D_MODEL * 4

        raw = place("raw", [P, RAW_SLOTS, CHUNK], F32, RAW_AT)
        w_hi = place("w_hi", [P, HALF_SLOTS, HALF], F32R, HI_AT)
        w_lo = place("w_lo", [P, HALF_SLOTS, HALF], F32R, LO_AT)
        xt = place("xt", [P, KT, 2, SEQ], F32R, XT_AT)
        nat = place("nat", [P, TT, PROJ_W], F32, NAT0_AT)
        x_in = place("x_in", [P, TT, D_MODEL], F32, X_AT)

        decay_sb = place("decay_sb", [P, RET_HEADS, 2 * P], F32, X_AT)
        rope_sb = place("rope_sb", [P, 2, 2, TT, 64], F32, X_AT + 8192)
        qk_rot = place("qk_rot", [P, 2, TT, P], F32, X_AT + 10240)
        swa_qk = place("swa_qk", [P, 2, TT, P], F32, X_AT + 12288)
        swa_qk_t = place("swa_qk_t", [P, 2, SEQ], F32, X_AT + 14336)
        gs0, gs1 = NAT0_AT + GS_AT * 4, NAT1_AT + GS_AT * 4
        rot_tmp = place("rot_tmp", [P, 4, 2, TT, 64], F32, gs0)
        qk_t = place("qk_t", [P, 2, SEQ], F32, gs0 + 4096)
        ret_s = place("ret_s", [P, 3 * P], F32, gs0 + 6144)
        swa_p = place("swa_p", [P, 2, 3 * P], F32, gs1)
        swa_pt = place("swa_pt", [P, 2, 3 * P], F32, gs1 + 3072)
        band_sb = place("band_sb", [P, 3 * P], F32, gs1 + 6144)
        gate_t = place("gate_t", [P, 2, TT, NB], F32, NAT0_AT + RQ_AT * 4)
        swa_xt = place("swa_xt", [P, 8, 2, SEQ], F32R, X_AT)
        mix_t = place("mix_t", [P, 2, PROJ_W], F32R, NAT0_AT)
        gain_mix = place("gain_mix", [P, D_MODEL], F32, X_AT)
        x2 = place("x2", [P, TT, D_MODEL], F32, X_AT)
        y_t = place("y_t", [P, FF_TILES, SEQ], F32, NAT0_AT)
        y_split = place("y_split", [P, 2, 4, 2, SEQ], F32R, NAT1_AT)
        gain_ffn = place("gain_ffn", [P, D_MODEL], F32, NAT1_AT + 16384)
        up_lo = place("up_lo", [P, 4, SEQ], F32, NAT1_AT + 24576)
        up_pad = place("up_pad", [P, 4, SEQ + 2], F32, NAT1_AT + 28672)
        conv_o = place("conv_o", [P, 4, SEQ], F32, NAT1_AT + 32800)
        gelu_o = place("gelu_o", [P, 2, SEQ], F32, NAT1_AT + 36896)
        y_out = place("y_out", [P, TT, D_MODEL], F32, NAT1_AT + 24576)

        small = [SMALL_AT]

        def tile(name, shape):
            at, size = small[0], 4 * int(np.prod(shape[1:]))
            small[0] += (size + 31) // 32 * 32
            return place(name, shape, F32, at)

        ident_sb = tile("ident_sb", [P, P])
        g_pre_sb = tile("g_pre_sb", [P, KT])
        g_ffn_sb = tile("g_ffn_sb", [P, KT])
        sinks_sb = tile("sinks_sb", [P, 2 * SWA_HEADS])
        conv_sb = tile("conv_sb", [P, 2 * FF_TILES, 4])
        x_ss = tile("x_ss", [P, TT])
        x_rms = tile("x_rms", [P, TT])
        ret_ss = tile("ret_ss", [P, RET_HEADS, TT])
        ret_rms = tile("ret_rms", [P, RET_HEADS, TT])
        swa_mx = tile("swa_mx", [P, 4])
        swa_m = tile("swa_m", [P, 4])
        swa_neg = tile("swa_neg", [P, 4])
        swa_sd = tile("swa_sd", [P, 4])
        swa_sum = tile("swa_sum", [P, 4])
        swa_se = tile("swa_se", [P, 4])
        swa_den = tile("swa_den", [P, 4])
        swa_rden = tile("swa_rden", [P, 4])
        out_ss = tile("out_ss", [P, TT, 4])
        tot_ss = tile("tot_ss", [P, TT])
        out_rms = tile("out_rms", [P, TT])
        x2_ss = tile("x2_ss", [P, TT])
        x2_rms = tile("x2_rms", [P, TT])
        down_ss = tile("down_ss", [P, TT, 4])
        rs_v = tile("rs_v", [P, RET_HEADS * TT])
        rs_t = tile("rs_t", [P, RET_HEADS * TT])
        diag = place("diag", [P, TT, P], F32, NAT0_AT + RG_AT * 4 - 2048)

        ps = ctx.enter_context(nc.psum_tensor("ps", [P, 8, NB], F32))

        x_landed = [sem(f"x_landed{i}") for i in range(8)]
        first_landed = [sem(f"first_landed{i}") for i in range(8)]
        small_landed = [sem(f"small_landed{i}") for i in range(5)]
        tables_landed = [sem(f"tables_landed{i}") for i in range(3)]
        x_again_landed = sem("x_again_landed")
        gain_mix_landed = sem("gain_mix_landed")
        gain_ffn_landed = sem("gain_ffn_landed")
        raw_landed = [sem(f"raw_landed{i}") for i in range(RAW_SLOTS)]
        hi_ready = sem("hi_ready")
        lo_ready = sem("lo_ready")
        weights_used = sem("weights_used")
        fill_done = sem("fill_done")
        fill_hi = sem("fill_hi")
        fill_lo = sem("fill_lo")
        order = sem("order")
        x_squared = sem("x_squared")
        x_rms_ready = sem("x_rms_ready")
        z_free = sem("z_free")
        pool_order = sem("pool_order")
        qk_rotated = sem("qk_rotated")
        swa_staged = sem("swa_staged")
        ret_t_done = sem("ret_t_done")
        ret_t_copied = sem("ret_t_copied")
        ret_s_done = sem("ret_s_done")
        ret_masked = sem("ret_masked")
        ret_av_done = sem("ret_av_done")
        ret_out = sem("ret_out")
        swa_t_done = sem("swa_t_done")
        swa_t_copied = sem("swa_t_copied")
        swa_s_done = sem("swa_s_done")
        swa_max = sem("swa_max")
        swa_exp = sem("swa_exp")
        swa_pt_done = sem("swa_pt_done")
        swa_pt_copied = sem("swa_pt_copied")
        swa_av_done = sem("swa_av_done")
        swa_out = sem("swa_out")
        gate_tanh = sem("gate_tanh")
        ret_gated = sem("ret_gated")
        swa_gate_tanh = sem("swa_gate_tanh")
        swa_merged = sem("swa_merged")
        mixed_ready = sem("mixed_ready")
        out_squared = sem("out_squared")
        out_scaled = sem("out_scaled")
        x2_ready = sem("x2_ready")
        x2_squared = sem("x2_squared")
        diag_ready = sem("diag_ready")
        up_low = sem("up_low")
        up_free = sem("up_free")
        tap0 = sem("tap0")
        taps = sem("taps")
        gelu = sem("gelu")
        y_ready = sem("y_ready")
        y_hi = sem("y_hi")
        y_lo = sem("y_lo")
        down_squared = sem("down_squared")
        result = sem("result")
        stored = sem("stored")

        def pair(f):
            return ps[:, fill_bank(f), :].rearrange("p (q t) -> p q t", q=2)

        def mix_view(kt, n, part):
            at = (kt % 8) * 2 * SEQ
            v = mix_t[:, kt // 8, at:at + n * 2 * SEQ].rearrange("p (q l t) -> p q l t", q=n, l=2)
            return v[:, :, part, :]

        def fill_target(f, part):
            if FILL_MIX <= f < FILL_H2:
                return mix_view((f - FILL_MIX) * 2, 2, part)
            target, start = ((xt, FILL_H) if f < FILL_SWA else (swa_xt, FILL_SWA) if f < FILL_RET
                             else (xt, FILL_RET) if f < FILL_MIX else (xt, FILL_H2))
            b = (f - start) * 2
            return target[:, b:b + 2, part, :]

        block = ctx.enter_context(nc.Block())

        @block.sync
        def _(sp):
            xv = x.rearrange("(t p) n -> p t n", p=P)
            wv = weights.rearrange("(g j) p n -> g j p n", j=RAW_SLOTS)
            for k in range(8):
                cols, part = slice(2 * P * k, 2 * P * (k + 1)), slice(k % 2 * HALF, (k % 2 + 1) * HALF)
                sp.dma_start(x_in[:, :, cols], xv[:, :, cols]).then_inc(x_landed[k], 16)
                sp.dma_start(raw[:, k // 2, part], wv[0, k // 2][:, part]).then_inc(first_landed[k], 16)
            with sp.Fori(1, GROUPS) as g:
                for j in range(RAW_SLOTS):
                    sp.wait_ge(lo_ready, 8 * g + 2 * j - 6)
                    sp.dma_start(raw[:, j, :], wv[bass.ds(g, 1), j].rearrange("a p n -> p (a n)"))\
                      .then_inc(raw_landed[j], 16)
            ov = out.rearrange("(t p) n -> p t n", p=P)
            for t in range(TT):
                for c in range(2):
                    cols = slice(c * 1024, (c + 1) * 1024)
                    sp.wait_ge(result, 2 * t + c + 1)
                    sp.dma_start(ov[:, t, cols], y_out[:, t, cols]).then_inc(stored, 16)
            sp.wait_ge(stored, 16 * 2 * TT)

        @block.gpsimd
        def _(pool):
            for k, (dst, src) in enumerate(((ident_sb, ident), (g_pre_sb, g_pre), (g_ffn_sb, g_ffn),
                                            (sinks_sb, sinks), (conv_sb, conv))):
                pool.dma_start(dst[:], src).then_inc(small_landed[k], 16)
            pool.wait_ge(fill_done, FILL_H + KT // 2)
            pool.wait_ge(x_rms_ready, 1)
            for k, (dst, src) in enumerate(((decay_sb, decay), (rope_sb, rope), (band_sb, band))):
                pool.dma_start(dst[:], src).then_inc(tables_landed[k], 16)
            pool.wait_ge(tables_landed[1], 16)
            pool.wait_ge(z_free, 6)

            qk = nat[:, :, RQ_AT:RV_AT].rearrange("p t (w c) -> p w t c", w=2)
            step = [0]

            def rotate(s):
                lo = qk[:, :, :, bass.ds(RET_DK * s, 64)]
                hi = qk[:, :, :, bass.ds(RET_DK * s + 64, 64)]
                for n, (half, table) in enumerate(((lo, 0), (hi, 1), (lo, 1), (hi, 0))):
                    last = pool.tensor_tensor(rot_tmp[:, n], half, rope_sb[:, table], ALU.mult)
                last.then_inc(pool_order, 1)
                pool.wait_ge(pool_order, s + 1)
                pool.tensor_tensor(qk_rot[:, :, :, 0:64], rot_tmp[:, 0], rot_tmp[:, 1], ALU.subtract)
                pool.tensor_tensor(qk_rot[:, :, :, 64:128], rot_tmp[:, 2], rot_tmp[:, 3], ALU.add)\
                    .then_inc(qk_rotated, 1)

            def stage(s, kv, with_k):
                last = pool.tensor_copy(swa_qk[:, 0], nat[:, :, bass.ds(SQ_AT + P * s, P)])
                for a in range(2 * with_k):
                    last = pool.tensor_copy(swa_qk[:, 1, :, 64 * a:64 * a + 64],
                                            nat[:, :, bass.ds(SK_AT + SWA_DH * kv, SWA_DH)])
                last.then_inc(swa_staged, 1)

            def heads(i, first):
                for u in range(2):
                    s = 2 * i + u
                    if not (first and u == 0):
                        pool.wait_ge(ret_t_done, s)
                        pool.wait_ge(qk_rotated, s)
                    rotate(s)
                    if first:
                        pool.wait_ge(z_free, 11 + u)
                    if not (first and u == 0):
                        pool.wait_ge(swa_t_done, s)
                    stage(s, i, u == 0)

            heads(0, True)
            with pool.Fori(1, 4) as i:
                heads(i, False)
            pool.wait_ge(ret_gated, 4)
            pool.dma_start(nat[:, :, RG_AT:GR_AT], x.rearrange("(t p) n -> p t n", p=P))\
                .then_inc(x_again_landed, 16)
            pool.wait_ge(weights_used, H_OUT)
            pool.dma_start(gain_mix[:], g_post_mix).then_inc(gain_mix_landed, 16)
            pool.wait_ge(fill_done, FILL_H2 + 8)
            pool.dma_start(gain_ffn[:], g_post_ffn).then_inc(gain_ffn_landed, 16)

        @block.scalar
        def _(act):
            def split_hi(g, k):
                if isinstance(g, int) and g == 0:
                    act.wait_ge(first_landed[k], 16)
                elif k % 2 == 0:
                    act.wait_ge(raw_landed[k // 2], 16 * g)
                if not (isinstance(g, int) and 8 * g + k < HALF_SLOTS):
                    act.wait_ge(weights_used, 8 * g + k - (HALF_SLOTS - 1))
                nc.scalar.activation(w_hi[:, k % HALF_SLOTS, :],
                                     raw[:, k // 2, (k % 2) * HALF:(k % 2 + 1) * HALF],
                                     ACT.Copy).then_inc(hi_ready, 1)

            def high(f, scale=1.0, gain=None):
                act.wait_ge(fill_done, f + 1)
                if gain is None:
                    nc.scalar.activation(fill_target(f, 0), pair(f), ACT.Copy, scale=scale)\
                        .then_inc(fill_hi, 1)
                    return
                kt = 2 * (f % 8) if f < FILL_H2 else 2 * (f - FILL_H2)
                for q in range(2):
                    last = nc.scalar.activation(fill_target(f, 0)[:, q, :], pair(f)[:, q, :], ACT.Copy,
                                                scale=gain[:, kt + q:kt + q + 1])
                last.then_inc(fill_hi, 1)

            def evict(m, bank):
                act.wait_ge(weights_used, 8 * m + 8)
                for t in range(TT):
                    last = nc.scalar.activation(nat[:, t, bass.ds(NB * m, NB)], ps[:, bank + t, :],
                                                ACT.Copy, scale=x_rms[:, t:t + 1])
                last.then_inc(z_free, 1)

            act.wait_ge(small_landed[1], 16)
            for k in range(8):
                high(FILL_H + k, gain=g_pre_sb)
                split_hi(0, k)
            nc.scalar.activation(nat[:, 1, GS_AT:PROJ_W], x_in[:, 1, :], ACT.Square,
                                 accum_out=x_ss[:, 1:2]).then_inc(x_squared, 1)
            nc.scalar.activation(swa_se[:, 0:1], g_pre_sb[:, 0:1], ACT.Copy).then_inc(z_free, 1)
            act.wait_ge(x_rms_ready, 1)

            with act.Fori(0, 5) as i:
                for u in range(2):
                    for k in range(8):
                        split_hi(2 * i + 1 + u, k)
                        if k == 3:
                            evict(2 * i + u, 2 * u)

            with act.Fori(0, 4) as i:
                for u in range(2):
                    s = 2 * i + u
                    for k in range(8):
                        split_hi(2 * i + 11 + u, k)
                        if k == 3:
                            evict(2 * i + 10 + u, 2 * u)
                            act.wait_ge(ret_t_done, s + 1)
                            nc.scalar.activation(qk_t[:], ps[:, 4, :].rearrange("p (w t) -> p w t", w=2),
                                                 ACT.Copy).then_inc(ret_t_copied, 1)
                            act.wait_ge(swa_t_done, s + 1)
                            new = SEQ * (2 - u)
                            nc.scalar.activation(swa_qk_t[:].rearrange("p w t -> p (w t)")[:, 0:new],
                                                 ps[:, 5, 0:new], ACT.Copy).then_inc(swa_t_copied, 1)
                        if k == 4:
                            act.wait_ge(swa_max, s + 1)
                            for a in range(2):
                                for t, cols in ((0, slice(0, P)), (1, slice(P, 3 * P))):
                                    j = 2 * a + t
                                    nc.scalar.activation(swa_p[:, a, cols], swa_p[:, a, cols], ACT.Exp,
                                                         bias=swa_neg[:, j:j + 1], scale=SWA_DH ** -0.5,
                                                         accum_out=swa_sum[:, j:j + 1])
                            nc.scalar.activation(swa_se[:], swa_sd[:], ACT.Exp).then_inc(swa_exp, 1)
                        if k == 6:
                            act.wait_ge(ret_av_done, s + 1)
                            for t in range(TT):
                                nc.scalar.activation(qk_t[:, t, :], ps[:, 4, t * RET_DV:(t + 1) * RET_DV],
                                                     ACT.Square, accum_out=ret_ss[:, bass.ds(s, 1), t])
                            nc.scalar.activation(nat[:, :, bass.ds(RV_AT + RET_DV * s, RET_DV)],
                                                 ps[:, 4, :].rearrange("p (t v) -> p t v", t=TT),
                                                 ACT.Copy).then_inc(ret_out, 1)
                        if k == 7:
                            act.wait_ge(swa_pt_done, s + 1)
                            for a in range(2):
                                last = nc.scalar.activation(swa_pt[:, a, :], ps[:, 7 - 2 * a, 0:3 * P], ACT.Copy)
                            last.then_inc(swa_pt_copied, 1)

            for j in range(4):
                for k in range(8):
                    split_hi(19 + j, k)
                    if k == 3:
                        evict(18 + j, 2 * (j % 2))
                        high(FILL_SWA + j)
                    if k == 4:
                        act.wait_ge(z_free, j + 17)
                        nc.scalar.activation(gate_t[:, j % 2], nat[:, :, RG_AT + NB * j:RG_AT + NB * (j + 1)],
                                             ACT.Tanh, scale=0.5).then_inc(gate_tanh, 1)
                    if k == 5:
                        gr = nat[:, :, GR_AT + NB * j:GR_AT + NB * (j + 1)]
                        nc.scalar.activation(gr, gr, ACT.Tanh, scale=0.5)

            for n in range(4):
                for k in range(12):
                    split_hi(G_MERGE + (12 * n + k) // 8, (12 * n + k) % 8)
                    if n == 0:
                        if k == 3:
                            evict(PROJ_BLOCKS - 1, 0)
                            act.wait_ge(weights_used, H_MERGE)
                        if 3 <= k <= 6:
                            high(FILL_RET + 2 * (k - 3))
                            high(FILL_RET + 2 * (k - 3) + 1)
                    elif k in (5, 6):
                        high(FILL_MIX + 2 * (n - 1) + k - 5, scale=0.5)
                    if k == 6:
                        act.wait_ge(z_free, PROJ_BLOCKS + 1)
                        gs = nat[:, :, GS_AT + NB * n:GS_AT + NB * (n + 1)]
                        nc.scalar.activation(gs, gs, ACT.Tanh, scale=0.5).then_inc(swa_gate_tanh, 1)

            def squares(half, done_at, dst, banks, ss, signal):
                act.wait_ge(weights_used, done_at)
                for b, bank in enumerate(banks):
                    nb = 2 * half + b
                    for t in range(TT):
                        nc.scalar.activation(dst(t, nb), ps[:, bank + t, :], ACT.Square,
                                             accum_out=ss[:, t, nb:nb + 1]).then_inc(signal, 1)

            def mixed_out(t, nb):
                return nat[:, t, GS_AT + NB * nb:GS_AT + NB * (nb + 1)]

            for p_ in range(2):
                for k in range(16):
                    split_hi(G_OUT + 2 * p_ + k // 8, k % 8)
                    if p_ == 0 and k in (5, 6):
                        high(FILL_MIX + 6 + k - 5, scale=0.5)
                    if p_ == 1 and k == 3:
                        act.wait_ge(mixed_ready, 4)
                        squares(0, H_OUT + 16, mixed_out, (2, 4), out_ss, out_squared)

            for k in range(4):
                split_hi(G_UP, k)
            squares(1, H_UP, mixed_out, (0, 6), out_ss, out_squared)
            for t in range(TT):
                act.wait_ge(x2_ready, t + 1)
                nc.scalar.activation(nat[:, t, GS_AT:PROJ_W], x2[:, t, :], ACT.Square,
                                     accum_out=x2_ss[:, t:t + 1]).then_inc(x2_squared, 1)
            act.wait_ge(small_landed[2], 16)
            for k in range(6):
                high(FILL_H2 + k, gain=g_ffn_sb)
            split_hi(G_UP, 4)
            for k in range(6, 8):
                high(FILL_H2 + k, gain=g_ffn_sb)
            for k in range(5, 8):
                split_hi(G_UP, k)

            def up_tile(i, f):
                return 2 * i + f if f < 2 else FF_TILES + 2 * i + f - 2

            def up_group_out(i, k, bank):
                if k == 3:
                    act.wait_ge(weights_used, H_UP + 8 * i + 8)
                    nc.scalar.activation(up_lo[:], ps[:, bank:bank + 4, SEQ:2 * SEQ], ACT.Copy)\
                        .then_inc(up_low, 1)
                if k == 4:
                    act.wait_ge(up_free, i + 2)
                    for f in range(4):
                        c = conv_sb[:, bass.ds(up_tile(i, f), 1), :]
                        last = nc.scalar.activation(conv_o[:, f, :], up_pad[:, f, 0:SEQ], ACT.Identity,
                                                    scale=c[:, 0, 0:1], bias=c[:, 0, 3:4])
                    last.then_inc(tap0, 1)
                if k == 6:
                    act.wait_ge(taps, i + 1)
                    nc.scalar.activation(gelu_o[:], conv_o[:, 2:4, :], ACT.Gelu_apprx_tanh)\
                        .then_inc(gelu, 1)

            act.wait_ge(small_landed[4], 16)
            with act.Fori(0, 10) as ii:
                for u in range(2):
                    for k in range(8):
                        split_hi(2 * ii + G_UP + 1 + u, k)
                        up_group_out(2 * ii + u, k, 4 * u)
            for k in range(8):
                split_hi(G_UP + 21, k)
                up_group_out(20, k, 0)

            def stage_hi(i, par):
                nc.scalar.activation(y_split[:, par, :, 0, :], y_t[:, bass.ds(4 * i, 4), :], ACT.Copy)\
                    .then_inc(y_hi, 1)

            act.wait_ge(y_ready, 2)
            stage_hi(0, 0)
            for k in range(8):
                split_hi(G_DOWN, k)
                up_group_out(21, k, 4)
            act.wait_ge(y_ready, UP_GROUPS)
            stage_hi(1, 1)
            with act.Fori(0, 4) as ii:
                for u in range(2):
                    i = 2 * ii + 1 + u
                    for k in range(8):
                        split_hi(2 * ii + G_DOWN + 1 + u, k)
                        if k == 4:
                            stage_hi(i + 1, u)
            for i in (9, 10):
                for k in range(8):
                    split_hi(G_DOWN + i, k)
                    if k == 4 and i == 9:
                        stage_hi(10, 0)
            for nb in range(4):
                act.wait_ge(weights_used, H_DOWN + 80 + 2 * nb + 2)
                for t in range(TT):
                    nc.scalar.activation(y_out[:, t, nb * NB:(nb + 1) * NB], ps[:, 2 * nb + t, :], ACT.Square,
                                         accum_out=down_ss[:, t, nb:nb + 1]).then_inc(down_squared, 1)

        @block.vector
        def _(dve):
            chain = [0]

            def link(ins):
                ins.then_inc(order, 1)
                chain[0] = chain[0] + 1
                dve.wait_ge(order, chain[0])

            def split_lo(g, k):
                dve.wait_ge(hi_ready, 8 * g + k + 1)
                nc.vector.tensor_tensor(w_lo[:, k % HALF_SLOTS, :],
                                        raw[:, k // 2, (k % 2) * HALF:(k % 2 + 1) * HALF],
                                        w_hi[:, k % HALF_SLOTS, :].bitcast(F32), ALU.subtract)\
                    .then_inc(lo_ready, 1)

            def low(f, scale=1.0, gain=None):
                dve.wait_ge(fill_hi, f + 1)
                hi = fill_target(f, 0).bitcast(F32)
                if gain is None:
                    nc.vector.scalar_tensor_tensor(out=fill_target(f, 1), in0=pair(f), scalar=scale, in1=hi,
                                                   op0=ALU.mult, op1=ALU.subtract).then_inc(fill_lo, 1)
                    return
                kt = 2 * (f % 8) if f < FILL_H2 else 2 * (f - FILL_H2)
                for q in range(2):
                    last = nc.vector.scalar_tensor_tensor(
                        out=fill_target(f, 1)[:, q, :], in0=pair(f)[:, q, :],
                        scalar=gain[:, kt + q:kt + q + 1], in1=hi[:, q, :],
                        op0=ALU.mult, op1=ALU.subtract)
                last.then_inc(fill_lo, 1)

            def rsqrt(y, ss, n, width):
                v, t = rs_v[:, 0:n], rs_t[:, 0:n]
                link(nc.vector.tensor_scalar(v, ss, 1.0 / width, EPS, ALU.mult, ALU.add))
                link(nc.vector.tensor_scalar(y.bitcast(I32), v.bitcast(I32), -0.5, RSQRT_MAGIC,
                                             ALU.mult, ALU.add))
                for _ in range(3):
                    link(nc.vector.tensor_tensor(t, y, y, ALU.mult))
                    link(nc.vector.tensor_tensor(t, t, v, ALU.mult))
                    link(nc.vector.tensor_scalar(t, t, -0.5, 1.5, ALU.mult, ALU.add))
                    link(nc.vector.tensor_tensor(y, y, t, ALU.mult))

            dve.wait_ge(small_landed[1], 16)
            for k in range(8):
                low(FILL_H + k, gain=g_pre_sb)
                split_lo(0, k)
            link(nc.vector.tensor_tensor_reduce(
                out=nat[:, 0, GS_AT:PROJ_W], in0=x_in[:, 0, :], in1=x_in[:, 0, :], scale=1.0,
                scalar=0.0, op0=ALU.mult, op1=ALU.add, accum_out=x_ss[:, 0:1]))
            dve.wait_ge(x_squared, 1)
            rsqrt(x_rms[:], x_ss[:], TT, D_MODEL)
            nc.vector.tensor_copy(x_ss[:], x_rms[:]).then_inc(x_rms_ready, 1)

            with dve.Fori(1, 11) as g:
                for k in range(8):
                    split_lo(g, k)

            dve.wait_ge(tables_landed[0], 16)
            dve.wait_ge(tables_landed[2], 16)
            dve.wait_ge(small_landed[3], 16)
            LINKS = 5
            start = chain[0]
            with dve.Fori(0, 4) as i:
                for u in range(2):
                    s = 2 * i + u
                    chain[0] = 2 * LINKS * i + (start + LINKS * u)
                    for k in range(8):
                        split_lo(2 * i + 11 + u, k)
                        if k == 3:
                            dve.wait_ge(ret_s_done, s + 1)
                            nc.vector.tensor_tensor(ret_s[:, 0:2 * P].rearrange("p (a n) -> p a n", a=1),
                                                    ps[:, 6:7, 0:2 * P],
                                                    decay_sb[:, bass.ds(s, 1), :], ALU.mult)
                            nc.vector.tensor_tensor(ret_s[:, 2 * P:3 * P].rearrange("p (a n) -> p a n", a=1),
                                                    ps[:, 6:7, 2 * P:3 * P],
                                                    decay_sb[:, bass.ds(s, 1), 0:P], ALU.mult)\
                                .then_inc(ret_masked, 1)
                            dve.wait_ge(swa_s_done, s + 1)
                            nc.vector.tensor_tensor(swa_p[:, 0, :], ps[:, 7, 0:3 * P], band_sb[:], ALU.add)
                            link(nc.vector.tensor_tensor(swa_p[:, 1, :], ps[:, 5, 0:3 * P], band_sb[:], ALU.add))
                            mx = swa_mx[:].rearrange("p (a t) -> p a t", a=2)
                            nc.vector.tensor_reduce(mx[:, :, 0], swa_p[:, :, 0:P], AX.X, ALU.max)
                            link(nc.vector.tensor_reduce(mx[:, :, 1], swa_p[:, :, P:3 * P], AX.X, ALU.max))
                            sink = sinks_sb[:, bass.ds(4 * s, 4)]
                            link(nc.vector.scalar_tensor_tensor(
                                out=swa_m[:], in0=swa_mx[:], scalar=SWA_DH ** -0.5, in1=sink,
                                op0=ALU.mult, op1=ALU.max))
                            nc.vector.tensor_scalar(swa_neg[:], swa_m[:], -1.0, None, ALU.mult)
                            nc.vector.tensor_tensor(swa_sd[:], sink, swa_m[:], ALU.subtract)\
                                .then_inc(swa_max, 1)
                        if k == 5:
                            dve.wait_ge(swa_exp, s + 1)
                            link(nc.vector.tensor_tensor(swa_den[:], swa_sum[:], swa_se[:], ALU.add))
                            link(nc.vector.reciprocal(swa_rden[:], swa_den[:]))
                    dve.wait_ge(swa_av_done, s + 1)
                    for a in range(2):
                        for t in range(TT):
                            j = 2 * a + t
                            last = nc.vector.tensor_scalar(
                                nat[:, t, bass.ds(SQ_AT + P * s + SWA_DH * a, SWA_DH)],
                                ps[:, 6, SWA_DH * j:SWA_DH * (j + 1)], swa_rden[:, j:j + 1], None, ALU.mult)
                    last.then_inc(swa_out, 1)
            chain[0] = start + 8 * LINKS

            dve.wait_ge(ret_out, RET_HEADS)
            rr = ret_rms[:].rearrange("p h t -> p (h t)")
            rsqrt(rr, ret_ss[:].rearrange("p h t -> p (h t)"), RET_HEADS * TT, RET_DV)
            link(nc.vector.tensor_scalar(rr, rr, 0.5, None, ALU.mult))
            for j in range(4):
                for k in range(8):
                    split_lo(19 + j, k)
                    if k == 3:
                        low(FILL_SWA + j)
                    if k == 4:
                        dve.wait_ge(gate_tanh, j + 1)
                        rg = nat[:, :, RG_AT + NB * j:RG_AT + NB * (j + 1)]
                        link(nc.vector.scalar_tensor_tensor(out=rg, in0=gate_t[:, j % 2], scalar=1.0, in1=rg,
                                                            op0=ALU.add, op1=ALU.mult))
                    if k == 6:
                        for a in range(2):
                            for t in range(TT):
                                at = NB * j + RET_DV * a
                                ret = nat[:, t, RV_AT + at:RV_AT + at + RET_DV]
                                last = nc.vector.scalar_tensor_tensor(
                                    out=ret, in0=ret, scalar=ret_rms[:, 2 * j + a, t:t + 1],
                                    in1=nat[:, t, RG_AT + at:RG_AT + at + RET_DV],
                                    op0=ALU.mult, op1=ALU.mult)
                        last.then_inc(ret_gated, 1)

            def gates(n):
                return (nat[:, :, GR_AT + NB * n:GR_AT + NB * (n + 1)],
                        nat[:, :, GS_AT + NB * n:GS_AT + NB * (n + 1)])

            def merge_swa(n):
                dve.wait_ge(weights_used, H_MERGE + 12 * n + 4)
                dve.wait_ge(swa_gate_tanh, n + 1)
                gs = gates(n)[1]
                nc.vector.scalar_tensor_tensor(out=gs, in0=gs, scalar=1.0, in1=ps[:, 2:4, :],
                                               op0=ALU.add, op1=ALU.mult).then_inc(swa_merged, 1)

            def merge_ret(n):
                dve.wait_ge(weights_used, H_MERGE + 12 * n + 12)
                gr, gs = gates(n)
                link(nc.vector.scalar_tensor_tensor(out=gr, in0=gr, scalar=1.0, in1=ps[:, 0:2, :],
                                                    op0=ALU.add, op1=ALU.mult))
                nc.vector.tensor_tensor(gr, gr, gs, ALU.add).then_inc(mixed_ready, 1)

            for n in range(4):
                for k in range(12):
                    split_lo(G_MERGE + (12 * n + k) // 8, (12 * n + k) % 8)
                    if n == 0:
                        if 3 <= k <= 6:
                            low(FILL_RET + 2 * (k - 3))
                            low(FILL_RET + 2 * (k - 3) + 1)
                    else:
                        if k == 3:
                            merge_ret(n - 1)
                        if k in (5, 6):
                            low(FILL_MIX + 2 * (n - 1) + k - 5, scale=0.5)
                    if k == 8:
                        merge_swa(n)

            def scale_out(half, banks):
                for b, bank in enumerate(banks):
                    nb = 2 * half + b
                    for t in range(TT):
                        dve.wait_ge(out_squared, 4 * half + 2 * b + t + 1)
                        nc.vector.tensor_tensor(nat[:, t, GS_AT + NB * nb:GS_AT + NB * (nb + 1)],
                                                ps[:, bank + t, :], gain_mix[:, NB * nb:NB * (nb + 1)],
                                                ALU.mult).then_inc(out_scaled, 1)

            for p_ in range(2):
                for k in range(16):
                    split_lo(G_OUT + 2 * p_ + k // 8, k % 8)
                    if p_ == 0:
                        if k == 3:
                            merge_ret(3)
                        if k in (5, 6):
                            low(FILL_MIX + 6 + k - 5, scale=0.5)
                    elif k == 5:
                        dve.wait_ge(gain_mix_landed, 16)
                        scale_out(0, (2, 4))

            for k in range(4):
                split_lo(G_UP, k)
            scale_out(1, (0, 6))
            link(nc.vector.tensor_reduce(tot_ss[:], out_ss[:], AX.X, ALU.add))
            rsqrt(out_rms[:], tot_ss[:], TT, D_MODEL)
            dve.wait_ge(x_again_landed, 16)
            dve.wait_ge(out_scaled, 8)
            for t in range(TT):
                nc.vector.scalar_tensor_tensor(out=x2[:, t, :], in0=nat[:, t, GS_AT:PROJ_W],
                                               scalar=out_rms[:, t:t + 1], in1=nat[:, t, RG_AT:GR_AT],
                                               op0=ALU.mult, op1=ALU.add).then_inc(x2_ready, 1)
            dve.wait_ge(x2_squared, 2)
            rsqrt(x2_rms[:], x2_ss[:], TT, D_MODEL)
            for t in range(TT):
                last = nc.vector.tensor_scalar(diag[:, t, :], ident_sb[:], x2_rms[:, t:t + 1], None, ALU.mult)
            last.then_inc(diag_ready, 1)
            for k in range(6):
                low(FILL_H2 + k, gain=g_ffn_sb)
            split_lo(G_UP, 4)
            for k in range(6, 8):
                low(FILL_H2 + k, gain=g_ffn_sb)
            for k in range(5, 8):
                split_lo(G_UP, k)
            nc.vector.memset(up_pad[:, :, 0:2], 0.0).then_inc(up_free, 1)

            def up_tile(i, f):
                return 2 * i + f if f < 2 else FF_TILES + 2 * i + f - 2

            UP_LINKS = 1

            def up_group_out(i, k, bank):
                if k == 3:
                    dve.wait_ge(up_low, i + 1)
                    nc.vector.tensor_tensor(up_pad[:, :, 2:SEQ + 2], ps[:, bank:bank + 4, 0:SEQ], up_lo[:],
                                            ALU.add).then_inc(up_free, 1)
                if k == 5:
                    dve.wait_ge(tap0, i + 1)
                    for tap in (1, 2):
                        for f in range(4):
                            last = nc.vector.scalar_tensor_tensor(
                                out=conv_o[:, f, :], in0=up_pad[:, f, tap:tap + SEQ],
                                scalar=conv_sb[:, bass.ds(up_tile(i, f), 1), tap], in1=conv_o[:, f, :],
                                op0=ALU.mult, op1=ALU.add)
                        if tap == 1:
                            link(last)
                    last.then_inc(taps, 1)
                if k == 7:
                    dve.wait_ge(gelu, i + 1)
                    nc.vector.tensor_tensor(y_t[:, bass.ds(2 * i, 2), :], conv_o[:, 0:2, :], gelu_o[:],
                                            ALU.mult).then_inc(y_ready, 1)

            start = chain[0]
            with dve.Fori(0, 10) as ii:
                for u in range(2):
                    chain[0] = 2 * UP_LINKS * ii + (start + UP_LINKS * u)
                    for k in range(8):
                        split_lo(2 * ii + G_UP + 1 + u, k)
                        up_group_out(2 * ii + u, k, 4 * u)
            chain[0] = start + 20 * UP_LINKS
            for k in range(8):
                split_lo(G_UP + 21, k)
                up_group_out(20, k, 0)

            def stage_lo(i, par):
                dve.wait_ge(y_hi, i + 1)
                nc.vector.tensor_tensor(y_split[:, par, :, 1, :], y_t[:, bass.ds(4 * i, 4), :],
                                        y_split[:, par, :, 0, :].bitcast(F32), ALU.subtract)\
                    .then_inc(y_lo, 1)

            stage_lo(0, 0)
            for k in range(8):
                split_lo(G_DOWN, k)
                up_group_out(21, k, 4)
            stage_lo(1, 1)
            with dve.Fori(0, 4) as ii:
                for u in range(2):
                    for k in range(8):
                        split_lo(2 * ii + G_DOWN + 1 + u, k)
                        if k == 4:
                            stage_lo(2 * ii + 2 + u, u)
            for i in (9, 10):
                for k in range(8):
                    split_lo(G_DOWN + i, k)
                    if k == 4 and i == 9:
                        stage_lo(10, 0)

            dve.wait_ge(gain_ffn_landed, 16)
            for nb in range(4):
                for t in range(TT):
                    dve.wait_ge(down_squared, 2 * nb + t + 1)
                    last = nc.vector.tensor_tensor(y_out[:, t, nb * NB:(nb + 1) * NB], ps[:, 2 * nb + t, :],
                                                   gain_ffn[:, nb * NB:(nb + 1) * NB], ALU.mult)
            link(last)
            link(nc.vector.tensor_reduce(tot_ss[:], down_ss[:], AX.X, ALU.add))
            rsqrt(out_rms[:], tot_ss[:], TT, D_MODEL)
            for t in range(TT):
                for c in range(2):
                    cols = slice(c * 1024, (c + 1) * 1024)
                    nc.vector.scalar_tensor_tensor(out=y_out[:, t, cols], in0=y_out[:, t, cols],
                                                   scalar=out_rms[:, t:t + 1], in1=x2[:, t, cols],
                                                   op0=ALU.mult, op1=ALU.add).then_inc(result, 1)

        @block.tensor
        def _(pe):
            mm = nc.tensor.matmul

            def products(h, k, left, bank, first, last, wait=None):
                if wait is not None:
                    pe.wait_ge(*wait)
                pe.wait_ge(lo_ready, h + 1)
                hi, lo = w_hi[:, k % HALF_SLOTS, :], w_lo[:, k % HALF_SLOTS, :]
                for q in range(2):
                    cols = slice(q * NB, (q + 1) * NB)
                    for t in range(TT):
                        o = ps[:, bank + t, :]
                        mm(o, left(q, 0, t), hi[:, cols], start=first and q == 0, stop=False,
                           skip_group_check=True)
                        mm(o, left(q, 0, t), lo[:, cols], start=False, stop=False, skip_group_check=True)
                        ins = mm(o, left(q, 1, t), hi[:, cols], start=False, stop=last and q == 1,
                                 skip_group_check=True)
                ins.then_inc(weights_used, 1)

            def from_xt(kt0):
                return lambda q, part, t: xt[:, kt0 + q, part, t * P:(t + 1) * P]

            def fill(f, source, diagonal=None):
                if f >= 4:
                    pe.wait_ge(fill_lo, f - 3)
                for q in range(2):
                    for t in range(TT):
                        o = ps[:, fill_bank(f), q * SEQ + t * P:q * SEQ + (t + 1) * P]
                        if diagonal is None:
                            ins = nc.tensor.transpose(o, source(q, t), ident_sb[:])
                        else:
                            ins = mm(o, source(q, t), diagonal[:, t, :], start=True, stop=True)
                ins.then_inc(fill_done, 1)

            def fill_x(b):
                pe.wait_ge(x_landed[b], 16)
                fill(FILL_H + b, lambda q, t: x_in[:, t, (2 * b + q) * P:(2 * b + q + 1) * P])

            pe.wait_ge(small_landed[0], 16)
            fill_x(0)
            for k in range(8):
                if k < 7:
                    fill_x(k + 1)
                products(k, k, from_xt(2 * k), 0, k == 0, k == 7, wait=(fill_lo, k + 1))

            def projection(m, k, bank):
                wait = (z_free, m) if k == 0 else None
                products(8 * m + k, k, from_xt(2 * k), bank, k == 0, k == 7, wait=wait)

            with pe.Fori(0, 5) as i:
                for u in range(2):
                    for k in range(8):
                        projection(2 * i + 1 + u, k, 2 * (1 - u))

            def transposes(s, with_k):
                pe.wait_ge(qk_rotated, s + 1)
                for w in range(2):
                    for t in range(TT):
                        at = w * SEQ + t * P
                        ins = nc.tensor.transpose(ps[:, 4, at:at + P], qk_rot[:, w, t, :], ident_sb[:])
                ins.then_inc(ret_t_done, 1)
                pe.wait_ge(swa_staged, s + 1)
                for w in range(1 + with_k):
                    for t in range(TT):
                        at = w * SEQ + t * P
                        ins = nc.tensor.transpose(ps[:, 5, at:at + P], swa_qk[:, w, t, :], ident_sb[:])
                ins.then_inc(swa_t_done, 1)

            def scores(s):
                pe.wait_ge(ret_t_copied, s + 1)
                mm(ps[:, 6, 0:SEQ], qk_t[:, 1, 0:P], qk_t[:, 0, :], start=True, stop=True)
                mm(ps[:, 6, SEQ:3 * P], qk_t[:, 1, P:SEQ], qk_t[:, 0, P:SEQ], start=True, stop=True)\
                    .then_inc(ret_s_done, 1)
                pe.wait_ge(swa_t_copied, s + 1)
                for a in range(2):
                    rows = slice(64 * a, 64 * a + 64)
                    mm(ps[:, 7 - 2 * a, 0:P], swa_qk_t[rows, 0, 0:P], swa_qk_t[rows, 1, 0:P],
                       start=True, stop=True)
                    ins = mm(ps[:, 7 - 2 * a, P:3 * P], swa_qk_t[rows, 0, P:SEQ], swa_qk_t[rows, 1, :],
                             start=True, stop=True)
                ins.then_inc(swa_s_done, 1)

            def retention_out(s):
                pe.wait_ge(ret_masked, s + 1)
                v = [nat[:, t, bass.ds(RV_AT + RET_DV * s, RET_DV)] for t in range(TT)]
                mm(ps[:, 4, 0:RET_DV], ret_s[:, 0:P], v[0], start=True, stop=True)
                mm(ps[:, 4, RET_DV:], ret_s[:, P:2 * P], v[0], start=True, stop=False)
                mm(ps[:, 4, RET_DV:], ret_s[:, 2 * P:3 * P], v[1], start=False, stop=True)\
                    .then_inc(ret_av_done, 1)

            def window_transposes(s):
                pe.wait_ge(swa_exp, s + 1)
                for a in range(2):
                    for j in range(3):
                        cols = slice(j * P, (j + 1) * P)
                        ins = nc.tensor.transpose(ps[:, 7 - 2 * a, cols], swa_p[:, a, cols], ident_sb[:])
                ins.then_inc(swa_pt_done, 1)

            def window_out(s, kv):
                pe.wait_ge(swa_pt_copied, s + 1)
                v = [nat[:, t, bass.ds(SV_AT + SWA_DH * kv, SWA_DH)] for t in range(TT)]
                for a in range(2):
                    o = [ps[:, 6, SWA_DH * (2 * a + t):SWA_DH * (2 * a + t + 1)] for t in range(TT)]
                    mm(o[0], swa_pt[:, a, 0:P], v[0], start=True, stop=True)
                    mm(o[1], swa_pt[:, a, P:2 * P], v[0], start=True, stop=False)
                    ins = mm(o[1], swa_pt[:, a, 2 * P:3 * P], v[1], start=False, stop=True)
                ins.then_inc(swa_av_done, 1)

            with pe.Fori(0, 4) as i:
                for u in range(2):
                    s = 2 * i + u
                    for k in range(8):
                        if k == 0:
                            transposes(s, u == 0)
                        if k == 1:
                            scores(s)
                        if k == 3:
                            retention_out(s)
                        if k == 4:
                            window_transposes(s)
                        if k == 5:
                            window_out(s, i)
                        projection(2 * i + 11 + u, k, 2 * (1 - u))

            def fill_heads(f):
                at = RV_AT + (f - FILL_RET) * 2 * P if f >= FILL_RET else SQ_AT + (f - FILL_SWA) * 2 * P
                fill(f, lambda q, t: nat[:, t, at + q * P:at + (q + 1) * P])

            pe.wait_ge(swa_out, SWA_HEADS // 2)
            for j in range(4):
                for k in range(8):
                    if k == 0:
                        fill_heads(FILL_SWA + j)
                    projection(19 + j, k, 2 * (1 - j % 2))

            def fill_mix(f):
                at = GR_AT + (f - FILL_MIX) * 2 * P
                pe.wait_ge(mixed_ready, (f - FILL_MIX) // 2 + 1)
                fill(f, lambda q, t: nat[:, t, at + q * P:at + (q + 1) * P])

            pe.wait_ge(ret_gated, 4)
            for n in range(4):
                for k in range(12):
                    if n == 0 and k < 4:
                        fill_heads(FILL_RET + 2 * k)
                        fill_heads(FILL_RET + 2 * k + 1)
                    if n > 0 and k in (2, 3):
                        fill_mix(FILL_MIX + 2 * (n - 1) + k - 2)
                    if k == 0:
                        pe.wait_ge(*((z_free, PROJ_BLOCKS) if n == 0 else (swa_merged, n)))
                    if k == 4:
                        pe.wait_ge(*((z_free, PROJ_BLOCKS + 1) if n == 0 else (mixed_ready, n)))
                    h = H_MERGE + 12 * n + k
                    if k < 4:
                        products(h, k, lambda q, part, t: swa_xt[:, 2 * k + q, part, t * P:(t + 1) * P],
                                 2, k == 0, k == 3, wait=(fill_lo, FILL_SWA + k + 1) if n == 0 else None)
                    else:
                        products(h, k, from_xt(2 * (k - 4)), 0, k == 4, k == 11,
                                 wait=(fill_lo, FILL_RET + k - 4 + 1) if n == 0 else None)

            for p_, banks in enumerate(((2, 4), (0, 6))):
                for k in range(16):
                    group, b, e = k // 4, k // 2 % 2, k % 2
                    kt0 = 4 * group + 2 * e
                    if p_ == 0 and k in (2, 3):
                        fill_mix(FILL_MIX + 6 + k - 2)
                    if k == 0:
                        pe.wait_ge(*((swa_merged, 4) if p_ == 0 else (mixed_ready, 4)))
                    if k == 2:
                        pe.wait_ge(fill_lo, FILL_MIX + 6 + 2 * p_)
                    products(H_OUT + 16 * p_ + k, k,
                             lambda q, part, t: mix_view(kt0 + q, 1, part)[:, 0, t * P:(t + 1) * P],
                             banks[b], group == 0 and e == 0, group == 3 and e == 1,
                             wait=(fill_lo, FILL_MIX + kt0 // 2 + 1) if p_ == 0 else None)

            def up_half(i, k, bank):
                if k == 0 and not (isinstance(i, int) and i == 0):
                    pe.wait_ge(up_free, i)
                pe.wait_ge(lo_ready, 8 * i + (H_UP + k + 1))
                hi, lo = w_hi[:, k % HALF_SLOTS, :], w_lo[:, k % HALF_SLOTS, :]
                kt0 = k % 4 * 4
                for q in range(4):
                    kt = kt0 + q
                    for f in range(2):
                        o = ps[:, bank + 2 * (k // 4) + f, :]
                        cols = slice(q * 2 * P + f * P, q * 2 * P + (f + 1) * P)
                        mm(o, hi[:, cols], xt[:, kt, :, :].rearrange("p l t -> p (l t)"),
                           start=kt == 0, stop=False, skip_group_check=True)
                        ins = mm(o[:, 0:SEQ], lo[:, cols], xt[:, kt, 0, :],
                                 start=False, stop=kt == KT - 1, skip_group_check=True)
                ins.then_inc(weights_used, 1)

            def fill_h2(b):
                fill(FILL_H2 + b, lambda q, t: x2[:, t, (2 * b + q) * P:(2 * b + q + 1) * P], diagonal=diag)

            pe.wait_ge(diag_ready, 1)
            for b in range(4):
                fill_h2(b)
            for k in range(8):
                if k in (1, 2):
                    fill_h2(2 * k + 2)
                    fill_h2(2 * k + 3)
                if k < 4:
                    pe.wait_ge(fill_lo, FILL_H2 + 2 * k + 2)
                up_half(0, k, 0)
            with pe.Fori(0, 10) as ii:
                for u in range(2):
                    for k in range(8):
                        up_half(2 * ii + 1 + u, k, 4 * (1 - u))
            for k in range(8):
                up_half(UP_GROUPS - 1, k, 4)

            def down(i, par, first, last):
                for k in range(8):
                    if k == 0:
                        pe.wait_ge(y_lo, i + 1)
                    if first and k in (0, 4):
                        pe.wait_ge(up_free, UP_GROUPS + k // 4)
                    e = k % 2
                    products(8 * i + (H_DOWN + k), k,
                             lambda q, part, t: y_split[:, par, 2 * e + q, part, t * P:(t + 1) * P],
                             2 * (k // 2), first and e == 0, last and e == 1)

            down(0, 0, True, False)
            with pe.Fori(0, 4) as ii:
                for u in range(2):
                    down(2 * ii + 1 + u, 1 - u, False, False)
            down(9, 1, False, False)
            down(10, 0, False, True)


def _tables():
    pos = np.arange(SEQ, dtype=np.float32)
    inv = (1.0 / (np.float32(10000.0) ** (np.arange(0, RET_DK, 2, dtype=np.float32) / RET_DK))).astype(np.float32)
    ang = (pos[:, None] * inv[None, :]).astype(np.float32)
    cs = np.stack([np.cos(ang), np.sin(ang)])
    cs = cs.reshape(2, TT, P, 64).transpose(2, 0, 1, 3)
    rope = np.ascontiguousarray(np.broadcast_to(cs[:, :, None], (P, 2, 2, TT, 64))).astype(np.float32)
    log_gamma = np.log(1.0 - 2.0 ** (-5.0 - np.arange(RET_HEADS, dtype=np.float64)))
    rel = np.arange(2 * P)[None, :] - np.arange(P)[:, None]
    decay = np.where(rel[:, None] >= 0, np.exp(log_gamma[None, :, None] * np.maximum(rel, 0)[:, None]), 0.0)
    decay = (decay * RET_DK ** -0.5).astype(np.float32)
    q, k = np.arange(P)[:, None], np.arange(P)[None, :]
    same = np.where(k <= q, 0.0, MASKED)
    before = np.where(k > q, 0.0, MASKED)
    band = np.concatenate([same, before, same], axis=1).astype(np.float32)
    return np.eye(P, dtype=np.float32), decay, rope, band


def _weight_stream(w_in, w_ret_o, w_swa_o, w_out, w_up, w_down):
    def blocks(w):
        k, n = w.shape
        return w.reshape(k // (4 * P), 4, P, n // NB, NB).transpose(3, 0, 2, 1, 4)

    order = [14, 0, 1, 2, 3, 4, 5, 6, 7, 12, 13, 8, 9, 10, 11, 15, 16, 17, 18, 19, 20, 21, 22]
    parts = [blocks(w_in)[order]]
    parts.append(np.concatenate([blocks(w_swa_o), blocks(w_ret_o)], axis=1))
    o = blocks(w_out)
    parts.append(o.reshape(2, 2, *o.shape[1:]).transpose(0, 2, 1, 3, 4, 5))
    up = w_up.reshape(2, 8, P, 2, UP_GROUPS, 256)
    parts.append(up.transpose(4, 3, 0, 2, 1, 5))
    down = w_down.reshape(DOWN_GROUPS, 4, P, 4, NB)
    parts.append(down.transpose(0, 3, 2, 1, 4))
    return np.concatenate([a.reshape(-1, P, CHUNK) for a in parts], axis=0)


def kernel(x, g_pre_mix, w_in, w_ret_o, w_swa_o, w_out, swa_sinks, g_post_mix,
           g_pre_ffn, w_up, conv_w, conv_b, w_down, g_post_ffn):
    import concourse.bacc as bacc
    from concourse.bass_utils import run_bass_kernel_spmd

    a = {k: np.asarray(v) for k, v in locals().items() if k not in ("bacc", "run_bass_kernel_spmd")}
    ident, decay, rope, band = _tables()
    arrays = {
        "weights": _weight_stream(a["w_in"][0], a["w_ret_o"][0], a["w_swa_o"][0], a["w_out"][0],
                                  a["w_up"][0], a["w_down"][0]),
        "x": a["x"][0],
        "g_pre": np.ascontiguousarray(a["g_pre_mix"][0].reshape(KT, P).T),
        "g_ffn": np.ascontiguousarray(a["g_pre_ffn"][0].reshape(KT, P).T),
        "g_post_mix": np.ascontiguousarray(np.broadcast_to(a["g_post_mix"][0], (P, D_MODEL))),
        "g_post_ffn": np.ascontiguousarray(np.broadcast_to(a["g_post_ffn"][0], (P, D_MODEL))),
        "sinks": np.ascontiguousarray(np.broadcast_to(np.repeat(a["swa_sinks"][0], TT), (P, TT * SWA_HEADS))),
        "conv": np.ascontiguousarray(np.concatenate([a["conv_w"][0], a["conv_b"]], axis=0)
                                     .reshape(4, 2 * FF_TILES, P).transpose(2, 1, 0)),
        "ident": ident, "decay": decay, "rope": rope, "band": band,
    }
    nc = bacc.Bacc("TRN2", target_bir_lowering=False, num_devices=1)
    args = {k: nc.dram_tensor(k, v.shape, mybir.dt.from_np(v.dtype), kind="ExternalInput").ap()
            for k, v in arrays.items()}
    out = nc.dram_tensor("out", (SEQ, D_MODEL), F32, kind="ExternalOutput").ap()
    build(nc, out=out, **args)
    r = run_bass_kernel_spmd(nc, [arrays], core_ids=[0])
    return r.results[0]["out"].reshape(1, SEQ, D_MODEL)
```

```python
from contextlib import ExitStack

import numpy as np

import concourse.bass as bass
from concourse import mybir

ALU = mybir.AluOpType
ACT = mybir.ActivationFunctionType
AX = mybir.AxisListType
F32 = mybir.dt.float32
F32R = mybir.dt.float32r
I32 = mybir.dt.int32

P = 128
D_MODEL = 2048
SEQ = 256
TT = SEQ // P
KT = D_MODEL // P
RET_HEADS, RET_DK, RET_DV = 8, 128, 256
SWA_HEADS, SWA_KV, SWA_DH, WINDOW = 16, 4, 64, 128
D_FF = 5632
EPS = 1e-6
NB = 512
CHUNK = 2048
HALF = CHUNK // 2
RAW_SLOTS = 4
HALF_SLOTS = 4

SK_AT = 0
SV_AT = SK_AT + SWA_KV * SWA_DH
RQ_AT = SV_AT + SWA_KV * SWA_DH
RK_AT = RQ_AT + RET_HEADS * RET_DK
RV_AT = RK_AT + RET_HEADS * RET_DK
SQ_AT = RV_AT + RET_HEADS * RET_DV
RG_AT = SQ_AT + SWA_HEADS * SWA_DH
GR_AT = RG_AT + RET_HEADS * RET_DV
GS_AT = GR_AT + D_MODEL
PROJ_W = GS_AT + D_MODEL
PROJ_BLOCKS = PROJ_W // NB

G_MERGE = PROJ_BLOCKS
G_OUT = G_MERGE + 6
G_UP = G_OUT + 4
UP_GROUPS = D_FF // 256
G_DOWN = G_UP + UP_GROUPS
DOWN_GROUPS = D_FF // (4 * P)
GROUPS = G_DOWN + DOWN_GROUPS
H_MERGE, H_OUT, H_UP, H_DOWN = (8 * g for g in (G_MERGE, G_OUT, G_UP, G_DOWN))
FF_TILES = D_FF // P

FILL_H = 0
FILL_SWA = FILL_H + KT // 2
FILL_RET = FILL_SWA + 4
FILL_MIX = FILL_RET + KT // 2
FILL_H2 = FILL_MIX + KT // 2

VECTOR_PIECES = ((0, 0, 256), (0, 256, 512), (0, 768, 512), (1, 0, 512), (1, 1536, 512), (1, 512, 512))
POOL_PIECES = ((0, 1280, 256), (0, 1536, 512), (1, 1024, 512))

VECTOR_X2 = ((0, 0), (1, 0), (0, 1), (1, 1), (1, 3))
POOL_X2 = ((0, 2), (1, 2), (0, 3))

MASKED = -3.0e38
RSQRT_MAGIC = float(0x5F3759DF - (3 << 23) - (1 << 31))


def fill_bank(f):
    return 4 + f % 4


def build(nc, weights, x, ident_g_pre, g_ffn, g_post_mix, g_post_ffn, sinks, conv, decay, rope, band, out):
    with ExitStack() as ctx:
        base = (nc.sbuf_base + 31) // 32 * 32

        def place(name, shape, dt, at):
            return nc.alloc_sbuf_tensor_at(name, shape, dt, offset=base + at)

        def sem(name):
            return ctx.enter_context(nc.semaphore(name))

        RAW_AT = 0
        HI_AT = RAW_AT + RAW_SLOTS * CHUNK * 4
        LO_AT = HI_AT + HALF_SLOTS * HALF * 4
        XT_AT = LO_AT + HALF_SLOTS * HALF * 4
        NAT0_AT = XT_AT + KT * 2 * SEQ * 4
        NAT1_AT = NAT0_AT + PROJ_W * 4
        X_AT = NAT1_AT + PROJ_W * 4
        SMALL_AT = X_AT + TT * D_MODEL * 4

        raw = place("raw", [P, RAW_SLOTS, CHUNK], F32, RAW_AT)
        w_hi = place("w_hi", [P, HALF_SLOTS, HALF], F32R, HI_AT)
        w_lo = place("w_lo", [P, HALF_SLOTS, HALF], F32R, LO_AT)
        xt = place("xt", [P, KT, 2, SEQ], F32R, XT_AT)
        nat = place("nat", [P, TT, PROJ_W], F32, NAT0_AT)
        x_in = place("x_in", [P, TT, D_MODEL], F32, X_AT)

        decay_sb = place("decay_sb", [P, RET_HEADS, 2 * P], F32, X_AT)
        rope_sb = place("rope_sb", [P, 2, 2, TT, 64], F32, X_AT + 8192)
        qk_rot = place("qk_rot", [P, 2, TT, P], F32, X_AT + 10240)
        swa_qk = place("swa_qk", [P, 2, TT, P], F32, X_AT + 12288)
        swa_qk_t = place("swa_qk_t", [P, 2, SEQ], F32, X_AT + 14336)
        gs0, gs1 = NAT0_AT + GS_AT * 4, NAT1_AT + GS_AT * 4
        rot_tmp = place("rot_tmp", [P, 4, 2, TT, 64], F32, gs0)
        qk_t = place("qk_t", [P, 2, SEQ], F32, gs0 + 4096)
        ret_s = place("ret_s", [P, 3 * P], F32, gs0 + 6144)
        swa_p = place("swa_p", [P, 2, 3 * P], F32, gs1)
        swa_pt = place("swa_pt", [P, 2, 3 * P], F32, gs1 + 3072)
        band_sb = place("band_sb", [P, 3 * P], F32, gs1 + 6144)
        gate_t = place("gate_t", [P, 2, TT, NB], F32, NAT0_AT + RQ_AT * 4)
        swa_xt = place("swa_xt", [P, 8, 2, SEQ], F32R, X_AT)
        mix_t = place("mix_t", [P, 2, PROJ_W], F32R, NAT0_AT)
        gain_mix = place("gain_mix", [P, D_MODEL], F32, X_AT + D_MODEL * 4)
        x2 = place("x2", [P, TT, D_MODEL], F32, X_AT)
        y_t = place("y_t", [P, FF_TILES, SEQ], F32, NAT0_AT)
        y_split = place("y_split", [P, 2, 4, 2, SEQ], F32R, NAT1_AT)
        gain_ffn = place("gain_ffn", [P, D_MODEL], F32, NAT1_AT + 16384)
        up_lo = place("up_lo", [P, 4, SEQ], F32, NAT1_AT + 24576)
        up_pad = place("up_pad", [P, 4, SEQ + 2], F32, NAT1_AT + 28672)
        conv_o = place("conv_o", [P, 4, SEQ], F32, NAT1_AT + 32800)
        gelu_o = place("gelu_o", [P, 2, SEQ], F32, NAT1_AT + 36896)
        x2_rms_b = place("x2_rms_b", [P, 4, SEQ], F32, NAT1_AT + 38944)
        y_out = place("y_out", [P, TT, D_MODEL], F32, NAT1_AT + 24576)

        small = [SMALL_AT]

        def tile(name, shape):
            at, size = small[0], 4 * int(np.prod(shape[1:]))
            small[0] += (size + 31) // 32 * 32
            return place(name, shape, F32, at)

        ident_g_pre_sb = tile("ident_g_pre_sb", [P, P + KT])
        ident_sb, g_pre_sb = ident_g_pre_sb[:, 0:P], ident_g_pre_sb[:, P:P + KT]
        ones = tile("ones", [P, P])
        g_ffn_sb = tile("g_ffn_sb", [P, KT])
        sinks_sb = tile("sinks_sb", [P, 2 * SWA_HEADS])
        conv_sb = tile("conv_sb", [P, 2 * FF_TILES, 4])
        x_ss = tile("x_ss", [P, TT, 8])
        x_rms = tile("x_rms", [P, TT])
        ret_ss = tile("ret_ss", [P, RET_HEADS, TT])
        ret_rms = tile("ret_rms", [P, RET_HEADS, TT])
        swa_mx = tile("swa_mx", [P, 4])
        swa_m = tile("swa_m", [P, 4])
        swa_neg = tile("swa_neg", [P, 4])
        swa_sd = tile("swa_sd", [P, 4])
        swa_sum = tile("swa_sum", [P, 4])
        swa_se = tile("swa_se", [P, 4])
        swa_den = tile("swa_den", [P, 4])
        swa_rden = tile("swa_rden", [P, 4])
        out_ss = tile("out_ss", [P, TT, 4])
        tot_ss = tile("tot_ss", [P, TT])
        out_rms = tile("out_rms", [P, TT])
        x2_ss = tile("x2_ss", [P, TT])
        x2_rms = tile("x2_rms", [P, TT])
        down_ss = tile("down_ss", [P, TT, 4])
        rs_v = tile("rs_v", [P, RET_HEADS * TT])
        rs_t = tile("rs_t", [P, RET_HEADS * TT])
        diag = place("diag", [P, TT, P], F32, NAT0_AT + RG_AT * 4 - 2048)

        ps = ctx.enter_context(nc.psum_tensor("ps", [P, 8, NB], F32))

        x_landed = [sem(f"x_landed{i}") for i in range(8)]
        first_landed = [sem(f"first_landed{i}") for i in range(8)]
        small_landed = [sem(f"small_landed{i}") for i in range(4)]
        tables_landed = [sem(f"tables_landed{i}") for i in range(3)]
        x_again_landed = sem("x_again_landed")
        gain_mix_landed = sem("gain_mix_landed")
        gain_ffn_landed = sem("gain_ffn_landed")
        raw_landed = [sem(f"raw_landed{i}") for i in range(RAW_SLOTS)]
        hi_ready = sem("hi_ready")
        lo_ready = sem("lo_ready")
        weights_used = sem("weights_used")
        fill_done = sem("fill_done")
        fill_hi = sem("fill_hi")
        fill_lo = sem("fill_lo")
        order = sem("order")
        ones_ready = sem("ones_ready")
        x_squared = sem("x_squared")
        x_rms_ready = sem("x_rms_ready")
        z_free = sem("z_free")
        pool_order = sem("pool_order")
        qk_rotated = sem("qk_rotated")
        swa_staged = sem("swa_staged")
        ret_t_done = sem("ret_t_done")
        ret_t_copied = sem("ret_t_copied")
        ret_s_done = sem("ret_s_done")
        ret_masked = sem("ret_masked")
        ret_av_done = sem("ret_av_done")
        ret_out = sem("ret_out")
        swa_t_done = sem("swa_t_done")
        swa_t_copied = sem("swa_t_copied")
        swa_s_done = sem("swa_s_done")
        swa_max = sem("swa_max")
        swa_exp = sem("swa_exp")
        swa_pt_done = sem("swa_pt_done")
        swa_pt_copied = sem("swa_pt_copied")
        swa_av_done = sem("swa_av_done")
        swa_out = sem("swa_out")
        gate_tanh = sem("gate_tanh")
        ret_gated = sem("ret_gated")
        swa_gate_tanh = sem("swa_gate_tanh")
        swa_merged = sem("swa_merged")
        mixed_ready = sem("mixed_ready")
        last_half_tile0 = sem("last_half_tile0")
        out_squared = sem("out_squared")
        x2_ready = sem("x2_ready")
        x2_scaled = sem("x2_scaled")
        x2_pool_ready = sem("x2_pool_ready")
        x2_squared = sem("x2_squared")
        diag_ready = sem("diag_ready")
        rms_spread = sem("rms_spread")
        rms_copied = sem("rms_copied")
        up_scaled = sem("up_scaled")
        up_low = sem("up_low")
        up_free = sem("up_free")
        tap0 = sem("tap0")
        taps = sem("taps")
        gelu = sem("gelu")
        y_ready = sem("y_ready")
        y_hi = sem("y_hi")
        y_lo = sem("y_lo")
        down_squared = sem("down_squared")
        out_scaled = sem("out_scaled")
        out_rms_ready = sem("out_rms_ready")
        piece_scaled = sem("piece_scaled")
        pool_result = sem("pool_result")
        pool_stored = sem("pool_stored")
        result = sem("result")
        stored = sem("stored")

        def pair(f):
            return ps[:, fill_bank(f), :].rearrange("p (q t) -> p q t", q=2)

        def mix_view(kt, n, part):
            at = (kt % 8) * 2 * SEQ
            v = mix_t[:, kt // 8, at:at + n * 2 * SEQ].rearrange("p (q l t) -> p q l t", q=n, l=2)
            return v[:, :, part, :]

        def fill_target(f, part):
            if FILL_MIX <= f < FILL_H2:
                return mix_view((f - FILL_MIX) * 2, 2, part)
            target, start = ((xt, FILL_H) if f < FILL_SWA else (swa_xt, FILL_SWA) if f < FILL_RET
                             else (xt, FILL_RET) if f < FILL_MIX else (xt, FILL_H2))
            b = (f - start) * 2
            return target[:, b:b + 2, part, :]

        block = ctx.enter_context(nc.Block())

        @block.sync
        def _(sp):
            xv = x.rearrange("(t p) n -> p t n", p=P)
            wv = weights.rearrange("(g j) p n -> g j p n", j=RAW_SLOTS)
            for k in range(8):
                cols, part = slice(2 * P * k, 2 * P * (k + 1)), slice(k % 2 * HALF, (k % 2 + 1) * HALF)
                sp.dma_start(x_in[:, :, cols], xv[:, :, cols]).then_inc(x_landed[k], 16)
                sp.dma_start(raw[:, k // 2, part], wv[0, k // 2][:, part]).then_inc(first_landed[k], 16)
            with sp.Fori(1, GROUPS) as g:
                for j in range(RAW_SLOTS):
                    sp.wait_ge(lo_ready, 8 * g + 2 * j - 6)
                    sp.dma_start(raw[:, j, :], wv[bass.ds(g, 1), j].rearrange("a p n -> p (a n)"))\
                      .then_inc(raw_landed[j], 16)
            ov = out.rearrange("(t p) n -> p t n", p=P)
            for n, (t, c, n_cols) in enumerate(VECTOR_PIECES):
                cols = slice(c, c + n_cols)
                sp.wait_ge(result, n + 1)
                sp.dma_start(ov[:, t, cols], y_out[:, t, cols]).then_inc(stored, 16)
            sp.wait_ge(stored, 16 * len(VECTOR_PIECES))
            sp.wait_ge(pool_stored, 16 * len(POOL_PIECES))

        @block.gpsimd
        def _(pool):
            for k, (dst, src) in enumerate(((g_ffn_sb, g_ffn), (sinks_sb, sinks), (conv_sb, conv))):
                pool.dma_start(dst[:], src).then_inc(small_landed[k + 1], 16)
            pool.wait_ge(fill_done, FILL_H + KT // 2)
            pool.wait_ge(x_rms_ready, 1)
            for k, (dst, src) in enumerate(((decay_sb, decay), (rope_sb, rope), (band_sb, band))):
                pool.dma_start(dst[:], src).then_inc(tables_landed[k], 16)
            pool.wait_ge(tables_landed[1], 16)
            pool.wait_ge(z_free, 6)

            qk = nat[:, :, RQ_AT:RV_AT].rearrange("p t (w c) -> p w t c", w=2)
            step = [0]

            def rotate(s):
                lo = qk[:, :, :, bass.ds(RET_DK * s, 64)]
                hi = qk[:, :, :, bass.ds(RET_DK * s + 64, 64)]
                for n, (half, table) in enumerate(((lo, 0), (hi, 1), (lo, 1), (hi, 0))):
                    last = pool.tensor_tensor(rot_tmp[:, n], half, rope_sb[:, table], ALU.mult)
                last.then_inc(pool_order, 1)
                pool.wait_ge(pool_order, s + 1)
                pool.tensor_tensor(qk_rot[:, :, :, 0:64], rot_tmp[:, 0], rot_tmp[:, 1], ALU.subtract)
                pool.tensor_tensor(qk_rot[:, :, :, 64:128], rot_tmp[:, 2], rot_tmp[:, 3], ALU.add)\
                    .then_inc(qk_rotated, 1)

            def stage(s, kv, with_k):
                last = pool.tensor_copy(swa_qk[:, 0], nat[:, :, bass.ds(SQ_AT + P * s, P)])
                for a in range(2 * with_k):
                    last = pool.tensor_copy(swa_qk[:, 1, :, 64 * a:64 * a + 64],
                                            nat[:, :, bass.ds(SK_AT + SWA_DH * kv, SWA_DH)])
                last.then_inc(swa_staged, 1)

            def heads(i, first):
                for u in range(2):
                    s = 2 * i + u
                    if not (first and u == 0):
                        pool.wait_ge(ret_t_done, s)
                        pool.wait_ge(qk_rotated, s)
                    rotate(s)
                    if first:
                        pool.wait_ge(z_free, 11 + u)
                    if not (first and u == 0):
                        pool.wait_ge(swa_t_done, s)
                    stage(s, i, u == 0)

            heads(0, True)
            with pool.Fori(1, 4) as i:
                heads(i, False)
            pool.wait_ge(ret_gated, 4)
            pool.dma_start(nat[:, :, RG_AT:GR_AT], x.rearrange("(t p) n -> p t n", p=P))\
                .then_inc(x_again_landed, 16)
            pool.wait_ge(weights_used, H_OUT)
            pool.dma_start(gain_mix[:], g_post_mix).then_inc(gain_mix_landed, 16)
            pool.wait_ge(x_again_landed, 16)
            for n, (t, c) in enumerate(POOL_X2):
                cols = slice(c * NB, (c + 1) * NB)
                pool.wait_ge(x2_scaled, n + 1)
                pool.tensor_tensor(x2[:, t, cols], nat[:, t, GS_AT:PROJ_W][:, cols],
                                   nat[:, t, RG_AT:GR_AT][:, cols], ALU.add).then_inc(x2_pool_ready, 1)
            pool.wait_ge(fill_done, FILL_H2 + 8)
            pool.dma_start(gain_ffn[:], g_post_ffn).then_inc(gain_ffn_landed, 16)

            pool.wait_ge(rms_copied, 1)

            def scale_group():
                pool.tensor_tensor(up_pad[:, :, 2:SEQ + 2], up_lo[:], x2_rms_b[:], ALU.mult)\
                    .then_inc(up_scaled, 1)

            pool.wait_ge(up_free, 2)
            scale_group()
            with pool.Fori(1, UP_GROUPS) as i:
                pool.wait_ge(up_free, i + 2)
                pool.wait_ge(taps, i)
                scale_group()

            for n, (t, c, n_cols) in enumerate(POOL_PIECES):
                cols = slice(c, c + n_cols)
                pool.wait_ge(piece_scaled, n + 1)
                pool.tensor_tensor(y_out[:, t, cols], y_out[:, t, cols], x2[:, t, cols], ALU.add)\
                    .then_inc(pool_result, 1)

        @block.scalar
        def _(act):
            def split_hi(g, k):
                if isinstance(g, int) and g == 0:
                    act.wait_ge(first_landed[k], 16)
                elif k % 2 == 0:
                    act.wait_ge(raw_landed[k // 2], 16 * g)
                if not (isinstance(g, int) and 8 * g + k < HALF_SLOTS):
                    act.wait_ge(weights_used, 8 * g + k - (HALF_SLOTS - 1))
                nc.scalar.activation(w_hi[:, k % HALF_SLOTS, :],
                                     raw[:, k // 2, (k % 2) * HALF:(k % 2 + 1) * HALF],
                                     ACT.Copy).then_inc(hi_ready, 1)

            def high(f, scale=1.0, gain=None):
                act.wait_ge(fill_done, f + 1)
                if gain is None:
                    nc.scalar.activation(fill_target(f, 0), pair(f), ACT.Copy, scale=scale)\
                        .then_inc(fill_hi, 1)
                    return
                kt = 2 * (f % 8) if f < FILL_H2 else 2 * (f - FILL_H2)
                for q in range(2):
                    last = nc.scalar.activation(fill_target(f, 0)[:, q, :], pair(f)[:, q, :], ACT.Copy,
                                                scale=gain[:, kt + q:kt + q + 1])
                last.then_inc(fill_hi, 1)

            def evict(m, bank):
                act.wait_ge(weights_used, 8 * m + 8)
                for t in range(TT):
                    last = nc.scalar.activation(nat[:, t, bass.ds(NB * m, NB)], ps[:, bank + t, :],
                                                ACT.Copy, scale=x_rms[:, t:t + 1])
                last.then_inc(z_free, 1)

            act.dma_start(ident_g_pre_sb[:], ident_g_pre).then_inc(small_landed[0], 16)
            act.wait_ge(ones_ready, 1)
            nc.scalar.activation(swa_m[:], ones[:, 0:4], ACT.Copy).then_inc(z_free, 1)

            act.wait_ge(small_landed[0], 16)
            for k in range(8):
                if k >= 2:
                    split_hi(0, k)
                high(FILL_H + k, gain=g_pre_sb)
                if k < 2:
                    split_hi(0, k)
                cols = slice(2 * P * k, 2 * P * (k + 1))
                last = nc.scalar.activation(nat[:, 1, GS_AT:PROJ_W][:, cols], x_in[:, 1, cols], ACT.Square,
                                            accum_out=x_ss[:, 1, k:k + 1])
            last.then_inc(x_squared, 1)

            with act.Fori(0, 5) as i:
                for u in range(2):
                    for k in range(8):
                        split_hi(2 * i + 1 + u, k)
                        if k == 3:
                            act.wait_ge(x_rms_ready, 1)
                            evict(2 * i + u, 2 * u)

            with act.Fori(0, 4) as i:
                for u in range(2):
                    s = 2 * i + u
                    for k in range(8):
                        split_hi(2 * i + 11 + u, k)
                        if k == 3:
                            evict(2 * i + 10 + u, 2 * u)
                            act.wait_ge(ret_t_done, s + 1)
                            nc.scalar.activation(qk_t[:], ps[:, 4, :].rearrange("p (w t) -> p w t", w=2),
                                                 ACT.Copy).then_inc(ret_t_copied, 1)
                            act.wait_ge(swa_t_done, s + 1)
                            new = SEQ * (2 - u)
                            nc.scalar.activation(swa_qk_t[:].rearrange("p w t -> p (w t)")[:, 0:new],
                                                 ps[:, 5, 0:new], ACT.Copy).then_inc(swa_t_copied, 1)
                        if k == 4:
                            act.wait_ge(swa_max, s + 1)
                            for a in range(2):
                                for t, cols in ((0, slice(0, P)), (1, slice(P, 3 * P))):
                                    j = 2 * a + t
                                    nc.scalar.activation(swa_p[:, a, cols], swa_p[:, a, cols], ACT.Exp,
                                                         bias=swa_neg[:, j:j + 1], scale=SWA_DH ** -0.5,
                                                         accum_out=swa_sum[:, j:j + 1])
                            nc.scalar.activation(swa_se[:], swa_sd[:], ACT.Exp).then_inc(swa_exp, 1)
                        if k == 6:
                            act.wait_ge(ret_av_done, s + 1)
                            for t in range(TT):
                                nc.scalar.activation(qk_t[:, t, :], ps[:, 4, t * RET_DV:(t + 1) * RET_DV],
                                                     ACT.Square, accum_out=ret_ss[:, bass.ds(s, 1), t])
                            nc.scalar.activation(nat[:, :, bass.ds(RV_AT + RET_DV * s, RET_DV)],
                                                 ps[:, 4, :].rearrange("p (t v) -> p t v", t=TT),
                                                 ACT.Copy).then_inc(ret_out, 1)
                        if k == 7:
                            act.wait_ge(swa_pt_done, s + 1)
                            for a in range(2):
                                last = nc.scalar.activation(swa_pt[:, a, :], ps[:, 7 - 2 * a, 0:3 * P], ACT.Copy)
                            last.then_inc(swa_pt_copied, 1)

            for j in range(4):
                for k in range(8):
                    split_hi(19 + j, k)
                    if k == 3:
                        evict(18 + j, 2 * (j % 2))
                        high(FILL_SWA + j)
                    if k == 4:
                        act.wait_ge(z_free, j + 17)
                        nc.scalar.activation(gate_t[:, j % 2], nat[:, :, RG_AT + NB * j:RG_AT + NB * (j + 1)],
                                             ACT.Tanh, scale=0.5).then_inc(gate_tanh, 1)
                    if k == 5:
                        gr = nat[:, :, GR_AT + NB * j:GR_AT + NB * (j + 1)]
                        nc.scalar.activation(gr, gr, ACT.Tanh, scale=0.5)

            for n in range(4):
                for k in range(12):
                    split_hi(G_MERGE + (12 * n + k) // 8, (12 * n + k) % 8)
                    if n == 0:
                        if k == 3:
                            evict(PROJ_BLOCKS - 1, 0)
                            act.wait_ge(weights_used, H_MERGE)
                        if 3 <= k <= 6:
                            high(FILL_RET + 2 * (k - 3))
                            high(FILL_RET + 2 * (k - 3) + 1)
                    elif k in (5, 6):
                        high(FILL_MIX + 2 * (n - 1) + k - 5, scale=0.5)
                    if k == 6:
                        act.wait_ge(z_free, PROJ_BLOCKS + 1)
                        gs = nat[:, :, GS_AT + NB * n:GS_AT + NB * (n + 1)]
                        nc.scalar.activation(gs, gs, ACT.Tanh, scale=0.5).then_inc(swa_gate_tanh, 1)

            def squares(t, nb, bank):
                nc.scalar.activation(nat[:, t, GR_AT + NB * nb:GR_AT + NB * (nb + 1)], ps[:, bank + t, :],
                                     ACT.Square, accum_out=out_ss[:, t, nb:nb + 1]).then_inc(out_squared, 1)

            for p_ in range(2):
                for k in range(16):
                    split_hi(G_OUT + 2 * p_ + k // 8, k % 8)
                    if p_ == 0 and k in (5, 6):
                        high(FILL_MIX + 6 + k - 5, scale=0.5)
                    if p_ == 1 and k == 3:
                        act.wait_ge(weights_used, H_OUT + 16)
                        for nb, bank in ((0, 2), (1, 4)):
                            for t in range(TT):
                                squares(t, nb, bank)

            for k in range(2):
                split_hi(G_UP, k)
            act.wait_ge(weights_used, H_UP - 2)
            for t in range(TT):
                squares(t, 2, 0)
            split_hi(G_UP, 2)
            act.wait_ge(last_half_tile0, 1)
            squares(0, 3, 2)
            act.wait_ge(weights_used, H_UP)
            squares(1, 3, 2)
            split_hi(G_UP, 3)
            act.wait_ge(out_rms_ready, 1)
            for t, c in POOL_X2:
                part = nat[:, t, GS_AT + NB * c:GS_AT + NB * (c + 1)]
                nc.scalar.activation(part, part, ACT.Copy, scale=out_rms[:, t:t + 1]).then_inc(x2_scaled, 1)
            act.wait_ge(small_landed[1], 16)
            for k in range(8):
                high(FILL_H2 + k, gain=g_ffn_sb)
                if k in (5, 7):
                    split_hi(G_UP, 4 + k // 7)
            act.wait_ge(x2_ready, len(VECTOR_X2))
            act.wait_ge(x2_pool_ready, len(POOL_X2))
            for t in range(TT):
                nc.scalar.activation(nat[:, t, GS_AT:PROJ_W], x2[:, t, :], ACT.Square,
                                     accum_out=x2_ss[:, t:t + 1]).then_inc(x2_squared, 1)
            for k in (6, 7):
                split_hi(G_UP, k)

            def up_tile(i, f):
                return 2 * i + f if f < 2 else FF_TILES + 2 * i + f - 2

            def up_group_out(i, k, bank):
                if k == 3:
                    act.wait_ge(weights_used, H_UP + 8 * i + 8)
                    nc.scalar.activation(up_lo[:], ps[:, bank:bank + 4, SEQ:2 * SEQ], ACT.Copy)\
                        .then_inc(up_low, 1)
                if k == 6:
                    act.wait_ge(up_scaled, i + 1)
                    for f in range(4):
                        c = conv_sb[:, bass.ds(up_tile(i, f), 1), :]
                        last = nc.scalar.activation(conv_o[:, f, :], up_pad[:, f, 0:SEQ], ACT.Identity,
                                                    scale=c[:, 0, 0:1], bias=c[:, 0, 3:4])
                    last.then_inc(tap0, 1)
                if k == 7:
                    act.wait_ge(taps, i + 1)
                    nc.scalar.activation(gelu_o[:], conv_o[:, 2:4, :], ACT.Gelu_apprx_tanh)\
                        .then_inc(gelu, 1)

            act.wait_ge(small_landed[3], 16)
            for k in range(8):
                split_hi(G_UP + 1, k)
                if k == 5:
                    act.wait_ge(rms_spread, 1)
                    for n in range(2):
                        last = nc.scalar.activation(x2_rms_b[:, 2 * n:2 * n + 2, :],
                                                    ps[:, 6, :].rearrange("p (f t) -> p f t", f=2), ACT.Copy)
                    last.then_inc(rms_copied, 1)
                up_group_out(0, k, 0)
            with act.Fori(0, 10) as ii:
                for u in range(2):
                    for k in range(8):
                        split_hi(2 * ii + G_UP + 2 + u, k)
                        up_group_out(2 * ii + 1 + u, k, 4 * (1 - u))

            def stage_hi(i, par):
                nc.scalar.activation(y_split[:, par, :, 0, :], y_t[:, bass.ds(4 * i, 4), :], ACT.Copy)\
                    .then_inc(y_hi, 1)

            act.wait_ge(y_ready, 2)
            stage_hi(0, 0)
            for k in range(8):
                split_hi(G_DOWN, k)
                up_group_out(21, k, 4)
            act.wait_ge(y_ready, UP_GROUPS)
            stage_hi(1, 1)
            with act.Fori(0, 4) as ii:
                for u in range(2):
                    i = 2 * ii + 1 + u
                    for k in range(8):
                        split_hi(2 * ii + G_DOWN + 1 + u, k)
                        if k == 4:
                            stage_hi(i + 1, u)
            for i in (9, 10):
                for k in range(8):
                    split_hi(G_DOWN + i, k)
                    if k == 4 and i == 9:
                        stage_hi(10, 0)
            for nb in range(4):
                for t in range(TT):
                    if nb == 3 and t == 0:
                        act.wait_ge(last_half_tile0, 2)
                    else:
                        act.wait_ge(weights_used, H_DOWN + 80 + 2 * nb + 2)
                    nc.scalar.activation(raw[:, nb, t * NB:(t + 1) * NB], ps[:, 2 * nb + t, :], ACT.Square,
                                         accum_out=down_ss[:, t, nb:nb + 1]).then_inc(down_squared, 1)
            act.wait_ge(out_rms_ready, 2)
            for t, c, n_cols in POOL_PIECES:
                cols = slice(c, c + n_cols)
                nc.scalar.activation(y_out[:, t, cols], y_out[:, t, cols], ACT.Copy,
                                     scale=out_rms[:, t:t + 1]).then_inc(piece_scaled, 1)
            for n, (t, c, n_cols) in enumerate(POOL_PIECES):
                cols = slice(c, c + n_cols)
                act.wait_ge(pool_result, n + 1)
                act.dma_start(out.rearrange("(t p) n -> p t n", p=P)[:, t, cols], y_out[:, t, cols])\
                    .then_inc(pool_stored, 16)

        @block.vector
        def _(dve):
            chain = [0]

            def link(ins):
                ins.then_inc(order, 1)
                chain[0] = chain[0] + 1
                dve.wait_ge(order, chain[0])

            def split_lo(g, k):
                dve.wait_ge(hi_ready, 8 * g + k + 1)
                nc.vector.tensor_tensor(w_lo[:, k % HALF_SLOTS, :],
                                        raw[:, k // 2, (k % 2) * HALF:(k % 2 + 1) * HALF],
                                        w_hi[:, k % HALF_SLOTS, :].bitcast(F32), ALU.subtract)\
                    .then_inc(lo_ready, 1)

            def low(f, scale=1.0, gain=None):
                dve.wait_ge(fill_hi, f + 1)
                hi = fill_target(f, 0).bitcast(F32)
                if gain is None:
                    nc.vector.scalar_tensor_tensor(out=fill_target(f, 1), in0=pair(f), scalar=scale, in1=hi,
                                                   op0=ALU.mult, op1=ALU.subtract).then_inc(fill_lo, 1)
                    return
                kt = 2 * (f % 8) if f < FILL_H2 else 2 * (f - FILL_H2)
                for q in range(2):
                    last = nc.vector.scalar_tensor_tensor(
                        out=fill_target(f, 1)[:, q, :], in0=pair(f)[:, q, :],
                        scalar=gain[:, kt + q:kt + q + 1], in1=hi[:, q, :],
                        op0=ALU.mult, op1=ALU.subtract)
                last.then_inc(fill_lo, 1)

            def rsqrt(y, ss, n, width, signal=None):
                v, t = rs_v[:, 0:n], rs_t[:, 0:n]
                link(nc.vector.tensor_scalar(v, ss, 1.0 / width, EPS, ALU.mult, ALU.add))
                link(nc.vector.tensor_scalar(y.bitcast(I32), v.bitcast(I32), -0.5, RSQRT_MAGIC,
                                             ALU.mult, ALU.add))
                for n_, scale in enumerate((64.0, 16.0, 4.0)):
                    link(nc.vector.scalar_tensor_tensor(out=t, in0=y, scalar=scale, in1=y,
                                                        op0=ALU.mult, op1=ALU.mult))
                    link(nc.vector.tensor_tensor(t, t, v, ALU.mult))
                    last = nc.vector.scalar_tensor_tensor(out=y, in0=t, scalar=-3.0, in1=y,
                                                          op0=ALU.add, op1=ALU.mult)
                    if n_ < 2 or signal is None:
                        link(last)
                    else:
                        last.then_inc(signal[0], 1)
                        dve.wait_ge(*signal)

            nc.vector.memset(ones[:], 1.0).then_inc(ones_ready, 1)
            dve.wait_ge(small_landed[0], 16)
            for k in range(8):
                if k >= 2:
                    split_lo(0, k)
                low(FILL_H + k, gain=g_pre_sb)
                if k < 2:
                    split_lo(0, k)
                cols = slice(2 * P * k, 2 * P * (k + 1))
                last = nc.vector.tensor_tensor_reduce(
                    out=nat[:, 0, GS_AT:PROJ_W][:, cols], in0=x_in[:, 0, cols], in1=x_in[:, 0, cols],
                    scale=1.0, scalar=0.0, op0=ALU.mult, op1=ALU.add, accum_out=x_ss[:, 0, k:k + 1])
            link(last)

            for k in range(8):
                split_lo(1, k)
                if k == 1:
                    dve.wait_ge(x_squared, 1)
                    link(nc.vector.tensor_reduce(tot_ss[:], x_ss[:], AX.X, ALU.add))
                    rsqrt(x_rms[:], tot_ss[:], TT, D_MODEL, signal=(x_rms_ready, 1))
            with dve.Fori(2, 11) as g:
                for k in range(8):
                    split_lo(g, k)

            dve.wait_ge(tables_landed[0], 16)
            dve.wait_ge(tables_landed[2], 16)
            dve.wait_ge(small_landed[2], 16)
            LINKS = 5
            start = chain[0]
            with dve.Fori(0, 4) as i:
                for u in range(2):
                    s = 2 * i + u
                    chain[0] = 2 * LINKS * i + (start + LINKS * u)
                    for k in range(8):
                        split_lo(2 * i + 11 + u, k)
                        if k == 3:
                            dve.wait_ge(ret_s_done, s + 1)
                            nc.vector.tensor_tensor(ret_s[:, 0:2 * P].rearrange("p (a n) -> p a n", a=1),
                                                    ps[:, 6:7, 0:2 * P],
                                                    decay_sb[:, bass.ds(s, 1), :], ALU.mult)
                            nc.vector.tensor_tensor(ret_s[:, 2 * P:3 * P].rearrange("p (a n) -> p a n", a=1),
                                                    ps[:, 6:7, 2 * P:3 * P],
                                                    decay_sb[:, bass.ds(s, 1), 0:P], ALU.mult)\
                                .then_inc(ret_masked, 1)
                            dve.wait_ge(swa_s_done, s + 1)
                            nc.vector.tensor_tensor(swa_p[:, 0, :], ps[:, 7, 0:3 * P], band_sb[:], ALU.add)
                            link(nc.vector.tensor_tensor(swa_p[:, 1, :], ps[:, 5, 0:3 * P], band_sb[:], ALU.add))
                            mx = swa_mx[:].rearrange("p (a t) -> p a t", a=2)
                            nc.vector.tensor_reduce(mx[:, :, 0], swa_p[:, :, 0:P], AX.X, ALU.max)
                            link(nc.vector.tensor_reduce(mx[:, :, 1], swa_p[:, :, P:3 * P], AX.X, ALU.max))
                            sink = sinks_sb[:, bass.ds(4 * s, 4)]
                            link(nc.vector.scalar_tensor_tensor(
                                out=swa_m[:], in0=swa_mx[:], scalar=SWA_DH ** -0.5, in1=sink,
                                op0=ALU.mult, op1=ALU.max))
                            nc.vector.tensor_scalar(swa_neg[:], swa_m[:], -1.0, None, ALU.mult)
                            nc.vector.tensor_tensor(swa_sd[:], sink, swa_m[:], ALU.subtract)\
                                .then_inc(swa_max, 1)
                        if k == 5:
                            dve.wait_ge(swa_exp, s + 1)
                            link(nc.vector.tensor_tensor(swa_den[:], swa_sum[:], swa_se[:], ALU.add))
                            link(nc.vector.reciprocal(swa_rden[:], swa_den[:]))
                    dve.wait_ge(swa_av_done, s + 1)
                    for a in range(2):
                        for t in range(TT):
                            j = 2 * a + t
                            last = nc.vector.tensor_scalar(
                                nat[:, t, bass.ds(SQ_AT + P * s + SWA_DH * a, SWA_DH)],
                                ps[:, 6, SWA_DH * j:SWA_DH * (j + 1)], swa_rden[:, j:j + 1], None, ALU.mult)
                    last.then_inc(swa_out, 1)
            chain[0] = start + 8 * LINKS

            dve.wait_ge(ret_out, RET_HEADS)
            rr = ret_rms[:].rearrange("p h t -> p (h t)")
            rsqrt(rr, ret_ss[:].rearrange("p h t -> p (h t)"), RET_HEADS * TT, RET_DV)
            link(nc.vector.tensor_scalar(rr, rr, 0.5, None, ALU.mult))
            for j in range(4):
                for k in range(8):
                    split_lo(19 + j, k)
                    if k == 3:
                        low(FILL_SWA + j)
                    if k == 4:
                        dve.wait_ge(gate_tanh, j + 1)
                        rg = nat[:, :, RG_AT + NB * j:RG_AT + NB * (j + 1)]
                        link(nc.vector.scalar_tensor_tensor(out=rg, in0=gate_t[:, j % 2], scalar=1.0, in1=rg,
                                                            op0=ALU.add, op1=ALU.mult))
                    if k == 6:
                        for a in range(2):
                            for t in range(TT):
                                at = NB * j + RET_DV * a
                                ret = nat[:, t, RV_AT + at:RV_AT + at + RET_DV]
                                last = nc.vector.scalar_tensor_tensor(
                                    out=ret, in0=ret, scalar=ret_rms[:, 2 * j + a, t:t + 1],
                                    in1=nat[:, t, RG_AT + at:RG_AT + at + RET_DV],
                                    op0=ALU.mult, op1=ALU.mult)
                        last.then_inc(ret_gated, 1)

            def gates(n):
                return (nat[:, :, GR_AT + NB * n:GR_AT + NB * (n + 1)],
                        nat[:, :, GS_AT + NB * n:GS_AT + NB * (n + 1)])

            def merge_swa(n):
                dve.wait_ge(weights_used, H_MERGE + 12 * n + 4)
                dve.wait_ge(swa_gate_tanh, n + 1)
                gs = gates(n)[1]
                nc.vector.scalar_tensor_tensor(out=gs, in0=gs, scalar=1.0, in1=ps[:, 2:4, :],
                                               op0=ALU.add, op1=ALU.mult).then_inc(swa_merged, 1)

            def merge_ret(n):
                dve.wait_ge(weights_used, H_MERGE + 12 * n + 12)
                gr, gs = gates(n)
                link(nc.vector.scalar_tensor_tensor(out=gr, in0=gr, scalar=1.0, in1=ps[:, 0:2, :],
                                                    op0=ALU.add, op1=ALU.mult))
                nc.vector.tensor_tensor(gr, gr, gs, ALU.add).then_inc(mixed_ready, 1)

            for n in range(4):
                for k in range(12):
                    split_lo(G_MERGE + (12 * n + k) // 8, (12 * n + k) % 8)
                    if n == 0:
                        if 3 <= k <= 6:
                            low(FILL_RET + 2 * (k - 3))
                            low(FILL_RET + 2 * (k - 3) + 1)
                    else:
                        if k == 3:
                            merge_ret(n - 1)
                        if k in (5, 6):
                            low(FILL_MIX + 2 * (n - 1) + k - 5, scale=0.5)
                    if k == 8:
                        merge_swa(n)

            def scale_out(t, nb, bank):
                dve.wait_ge(out_squared, 2 * nb + t + 1)
                return nc.vector.tensor_tensor(nat[:, t, GS_AT + NB * nb:GS_AT + NB * (nb + 1)],
                                               ps[:, bank + t, :], gain_mix[:, NB * nb:NB * (nb + 1)],
                                               ALU.mult)

            for p_ in range(2):
                for k in range(16):
                    split_lo(G_OUT + 2 * p_ + k // 8, k % 8)
                    if p_ == 0:
                        if k == 3:
                            merge_ret(3)
                        if k in (5, 6):
                            low(FILL_MIX + 6 + k - 5, scale=0.5)
                    elif k == 3:
                        dve.wait_ge(gain_mix_landed, 16)
                        for nb, bank in ((0, 2), (1, 4)):
                            for t in range(TT):
                                scale_out(t, nb, bank).then_inc(out_scaled, 1)

            for k in range(2):
                split_lo(G_UP, k)
            for t in range(TT):
                scale_out(t, 2, 0)
            split_lo(G_UP, 2)
            link(scale_out(0, 3, 2))
            dve.wait_ge(out_squared, 4 * TT)
            link(nc.vector.tensor_reduce(tot_ss[:], out_ss[:], AX.X, ALU.add))
            rsqrt(out_rms[:], tot_ss[:], TT, D_MODEL, signal=(out_rms_ready, 1))
            dve.wait_ge(x_again_landed, 16)

            def residual(t, c):
                cols = slice(c * NB, (c + 1) * NB)
                nc.vector.scalar_tensor_tensor(out=x2[:, t, cols], in0=nat[:, t, GS_AT:PROJ_W][:, cols],
                                               scalar=out_rms[:, t:t + 1],
                                               in1=nat[:, t, RG_AT:GR_AT][:, cols],
                                               op0=ALU.mult, op1=ALU.add).then_inc(x2_ready, 1)

            for t, c in VECTOR_X2[:4]:
                residual(t, c)
            for c in range(4):
                low(FILL_H2 + 2 * c, gain=g_ffn_sb)
                low(FILL_H2 + 2 * c + 1, gain=g_ffn_sb)
                if c == 1:
                    link(scale_out(1, 3, 2))
                    residual(*VECTOR_X2[4])
                if c > 0:
                    split_lo(G_UP, 2 + c)
            nc.vector.memset(up_pad[:, :, 0:2], 0.0).then_inc(up_free, 1)
            dve.wait_ge(x2_squared, 2)
            rsqrt(x2_rms[:], x2_ss[:], TT, D_MODEL)
            for t in range(TT):
                last = nc.vector.tensor_scalar(diag[:, t, :], ident_sb, x2_rms[:, t:t + 1], None, ALU.mult)
            last.then_inc(diag_ready, 1)
            for k in (6, 7):
                split_lo(G_UP, k)

            def up_tile(i, f):
                return 2 * i + f if f < 2 else FF_TILES + 2 * i + f - 2

            UP_LINKS = 1

            def up_group_out(i, k, bank):
                if k == 3:
                    dve.wait_ge(up_low, i + 1)
                    nc.vector.tensor_tensor(up_lo[:], ps[:, bank:bank + 4, 0:SEQ], up_lo[:],
                                            ALU.add).then_inc(up_free, 1)
                if k == 6:
                    dve.wait_ge(tap0, i + 1)
                    for tap in (1, 2):
                        for f in range(4):
                            last = nc.vector.scalar_tensor_tensor(
                                out=conv_o[:, f, :], in0=up_pad[:, f, tap:tap + SEQ],
                                scalar=conv_sb[:, bass.ds(up_tile(i, f), 1), tap], in1=conv_o[:, f, :],
                                op0=ALU.mult, op1=ALU.add)
                        if tap == 1:
                            link(last)
                    last.then_inc(taps, 1)
                if k == 7:
                    dve.wait_ge(gelu, i + 1)
                    nc.vector.tensor_tensor(y_t[:, bass.ds(2 * i, 2), :], conv_o[:, 0:2, :], gelu_o[:],
                                            ALU.mult).then_inc(y_ready, 1)

            start = chain[0]
            for k in range(8):
                split_lo(G_UP + 1, k)
                up_group_out(0, k, 0)
            with dve.Fori(0, 10) as ii:
                for u in range(2):
                    chain[0] = 2 * UP_LINKS * ii + (start + UP_LINKS * (1 + u))
                    for k in range(8):
                        split_lo(2 * ii + G_UP + 2 + u, k)
                        up_group_out(2 * ii + 1 + u, k, 4 * (1 - u))
            chain[0] = start + 21 * UP_LINKS

            def stage_lo(i, par):
                dve.wait_ge(y_hi, i + 1)
                nc.vector.tensor_tensor(y_split[:, par, :, 1, :], y_t[:, bass.ds(4 * i, 4), :],
                                        y_split[:, par, :, 0, :].bitcast(F32), ALU.subtract)\
                    .then_inc(y_lo, 1)

            stage_lo(0, 0)
            for k in range(8):
                split_lo(G_DOWN, k)
                up_group_out(21, k, 4)
            stage_lo(1, 1)
            with dve.Fori(0, 4) as ii:
                for u in range(2):
                    for k in range(8):
                        split_lo(2 * ii + G_DOWN + 1 + u, k)
                        if k == 4:
                            stage_lo(2 * ii + 2 + u, u)
            for i in (9, 10):
                for k in range(8):
                    split_lo(G_DOWN + i, k)
                    if k == 4 and i == 9:
                        stage_lo(10, 0)

            def scale_down(t, nb):
                dve.wait_ge(down_squared, 2 * nb + t + 1)
                return nc.vector.tensor_tensor(y_out[:, t, nb * NB:(nb + 1) * NB], ps[:, 2 * nb + t, :],
                                               gain_ffn[:, nb * NB:(nb + 1) * NB], ALU.mult)

            dve.wait_ge(gain_ffn_landed, 16)
            for nb in range(4):
                for t in range(TT):
                    if (nb, t) != (3, 1):
                        last = scale_down(t, nb)
            link(last)
            dve.wait_ge(down_squared, 4 * TT)
            link(nc.vector.tensor_reduce(tot_ss[:], down_ss[:], AX.X, ALU.add))
            rsqrt(out_rms[:], tot_ss[:], TT, D_MODEL, signal=(out_rms_ready, 2))
            for n, (t, c, n_cols) in enumerate(VECTOR_PIECES):
                cols = slice(c, c + n_cols)
                if n == 3:
                    link(scale_down(1, 3))
                nc.vector.scalar_tensor_tensor(out=y_out[:, t, cols], in0=y_out[:, t, cols],
                                               scalar=out_rms[:, t:t + 1], in1=x2[:, t, cols],
                                               op0=ALU.mult, op1=ALU.add).then_inc(result, 1)

        @block.tensor
        def _(pe):
            mm = nc.tensor.matmul

            def products(h, k, left, bank, first, last, wait=None, early=None):
                if wait is not None:
                    pe.wait_ge(*wait)
                pe.wait_ge(lo_ready, h + 1)
                hi, lo = w_hi[:, k % HALF_SLOTS, :], w_lo[:, k % HALF_SLOTS, :]
                for t in range(TT):
                    o = ps[:, bank + t, :]
                    for q in range(2):
                        cols = slice(q * NB, (q + 1) * NB)
                        mm(o, left(q, 0, t), hi[:, cols], start=first and q == 0, stop=False,
                           skip_group_check=True)
                        mm(o, left(q, 0, t), lo[:, cols], start=False, stop=False, skip_group_check=True)
                        ins = mm(o, left(q, 1, t), hi[:, cols], start=False, stop=last and q == 1,
                                 skip_group_check=True)
                    if early is not None and t == 0:
                        ins.then_inc(early, 1)
                ins.then_inc(weights_used, 1)

            def from_xt(kt0):
                return lambda q, part, t: xt[:, kt0 + q, part, t * P:(t + 1) * P]

            def fill(f, source):
                if f >= 4:
                    pe.wait_ge(fill_lo, f - 3)
                for q in range(2):
                    for t in range(TT):
                        o = ps[:, fill_bank(f), q * SEQ + t * P:q * SEQ + (t + 1) * P]
                        ins = nc.tensor.transpose(o, source(q, t), ident_sb)
                ins.then_inc(fill_done, 1)

            def fill_x(b):
                pe.wait_ge(x_landed[b], 16)
                fill(FILL_H + b, lambda q, t: x_in[:, t, (2 * b + q) * P:(2 * b + q + 1) * P])

            def keep_warm(n):
                for _ in range(n):
                    mm(ps[:, 7, 0:P], ones[:], ones[:], start=True, stop=True)

            def products_as_ready(k):
                hi, lo = w_hi[:, k, :], w_lo[:, k, :]
                left = from_xt(2 * k)
                for part, w, ready in ((0, hi, (hi_ready, k + 1)), (1, hi, (fill_lo, k + 1)),
                                       (0, lo, (lo_ready, k + 1))):
                    if part == 0 and w is hi:
                        pe.wait_ge(fill_hi, k + 1)
                    pe.wait_ge(*ready)
                    for t in range(TT):
                        for q in range(2):
                            ins = mm(ps[:, t, :], left(q, part, t), w[:, q * NB:(q + 1) * NB],
                                     start=k == 0 and q == 0 and part == 0 and w is hi, stop=False,
                                     skip_group_check=True)
                ins.then_inc(weights_used, 1)

            pe.wait_ge(ones_ready, 1)
            keep_warm(6)
            pe.wait_ge(small_landed[0], 16)
            fill_x(0)
            keep_warm(3)
            for k in range(8):
                if k < 7:
                    fill_x(k + 1)
                if k < 2:
                    products_as_ready(k)
                else:
                    products(k, k, from_xt(2 * k), 0, False, k == 7, wait=(fill_lo, k + 1))

            def projection(m, k, bank):
                wait = (z_free, m) if k == 0 else None
                products(8 * m + k, k, from_xt(2 * k), bank, k == 0, k == 7, wait=wait)

            with pe.Fori(0, 5) as i:
                for u in range(2):
                    for k in range(8):
                        projection(2 * i + 1 + u, k, 2 * (1 - u))

            def transposes(s, with_k):
                pe.wait_ge(qk_rotated, s + 1)
                for w in range(2):
                    for t in range(TT):
                        at = w * SEQ + t * P
                        ins = nc.tensor.transpose(ps[:, 4, at:at + P], qk_rot[:, w, t, :], ident_sb)
                ins.then_inc(ret_t_done, 1)
                pe.wait_ge(swa_staged, s + 1)
                for w in range(1 + with_k):
                    for t in range(TT):
                        at = w * SEQ + t * P
                        ins = nc.tensor.transpose(ps[:, 5, at:at + P], swa_qk[:, w, t, :], ident_sb)
                ins.then_inc(swa_t_done, 1)

            def scores(s):
                pe.wait_ge(ret_t_copied, s + 1)
                mm(ps[:, 6, 0:SEQ], qk_t[:, 1, 0:P], qk_t[:, 0, :], start=True, stop=True)
                mm(ps[:, 6, SEQ:3 * P], qk_t[:, 1, P:SEQ], qk_t[:, 0, P:SEQ], start=True, stop=True)\
                    .then_inc(ret_s_done, 1)
                pe.wait_ge(swa_t_copied, s + 1)
                for a in range(2):
                    rows = slice(64 * a, 64 * a + 64)
                    mm(ps[:, 7 - 2 * a, 0:P], swa_qk_t[rows, 0, 0:P], swa_qk_t[rows, 1, 0:P],
                       start=True, stop=True)
                    ins = mm(ps[:, 7 - 2 * a, P:3 * P], swa_qk_t[rows, 0, P:SEQ], swa_qk_t[rows, 1, :],
                             start=True, stop=True)
                ins.then_inc(swa_s_done, 1)

            def retention_out(s):
                pe.wait_ge(ret_masked, s + 1)
                v = [nat[:, t, bass.ds(RV_AT + RET_DV * s, RET_DV)] for t in range(TT)]
                mm(ps[:, 4, 0:RET_DV], ret_s[:, 0:P], v[0], start=True, stop=True)
                mm(ps[:, 4, RET_DV:], ret_s[:, P:2 * P], v[0], start=True, stop=False)
                mm(ps[:, 4, RET_DV:], ret_s[:, 2 * P:3 * P], v[1], start=False, stop=True)\
                    .then_inc(ret_av_done, 1)

            def window_transposes(s):
                pe.wait_ge(swa_exp, s + 1)
                for a in range(2):
                    for j in range(3):
                        cols = slice(j * P, (j + 1) * P)
                        ins = nc.tensor.transpose(ps[:, 7 - 2 * a, cols], swa_p[:, a, cols], ident_sb)
                ins.then_inc(swa_pt_done, 1)

            def window_out(s, kv):
                pe.wait_ge(swa_pt_copied, s + 1)
                v = [nat[:, t, bass.ds(SV_AT + SWA_DH * kv, SWA_DH)] for t in range(TT)]
                for a in range(2):
                    o = [ps[:, 6, SWA_DH * (2 * a + t):SWA_DH * (2 * a + t + 1)] for t in range(TT)]
                    mm(o[0], swa_pt[:, a, 0:P], v[0], start=True, stop=True)
                    mm(o[1], swa_pt[:, a, P:2 * P], v[0], start=True, stop=False)
                    ins = mm(o[1], swa_pt[:, a, 2 * P:3 * P], v[1], start=False, stop=True)
                ins.then_inc(swa_av_done, 1)

            with pe.Fori(0, 4) as i:
                for u in range(2):
                    s = 2 * i + u
                    for k in range(8):
                        if k == 0:
                            transposes(s, u == 0)
                        if k == 1:
                            scores(s)
                        if k == 3:
                            retention_out(s)
                        if k == 4:
                            window_transposes(s)
                        if k == 5:
                            window_out(s, i)
                        projection(2 * i + 11 + u, k, 2 * (1 - u))

            def fill_heads(f):
                at = RV_AT + (f - FILL_RET) * 2 * P if f >= FILL_RET else SQ_AT + (f - FILL_SWA) * 2 * P
                fill(f, lambda q, t: nat[:, t, at + q * P:at + (q + 1) * P])

            pe.wait_ge(swa_out, SWA_HEADS // 2)
            for j in range(4):
                for k in range(8):
                    if k == 0:
                        fill_heads(FILL_SWA + j)
                    projection(19 + j, k, 2 * (1 - j % 2))

            def fill_mix(f):
                at = GR_AT + (f - FILL_MIX) * 2 * P
                pe.wait_ge(mixed_ready, (f - FILL_MIX) // 2 + 1)
                fill(f, lambda q, t: nat[:, t, at + q * P:at + (q + 1) * P])

            pe.wait_ge(ret_gated, 4)
            for n in range(4):
                for k in range(12):
                    if n == 0 and k < 4:
                        fill_heads(FILL_RET + 2 * k)
                        fill_heads(FILL_RET + 2 * k + 1)
                    if n > 0 and k in (2, 3):
                        fill_mix(FILL_MIX + 2 * (n - 1) + k - 2)
                    if k == 0:
                        pe.wait_ge(*((z_free, PROJ_BLOCKS) if n == 0 else (swa_merged, n)))
                    if k == 4:
                        pe.wait_ge(*((z_free, PROJ_BLOCKS + 1) if n == 0 else (mixed_ready, n)))
                    h = H_MERGE + 12 * n + k
                    if k < 4:
                        products(h, k, lambda q, part, t: swa_xt[:, 2 * k + q, part, t * P:(t + 1) * P],
                                 2, k == 0, k == 3, wait=(fill_lo, FILL_SWA + k + 1) if n == 0 else None)
                    else:
                        products(h, k, from_xt(2 * (k - 4)), 0, k == 4, k == 11,
                                 wait=(fill_lo, FILL_RET + k - 4 + 1) if n == 0 else None)

            for p_, banks in enumerate(((2, 4), (0, 2))):
                for k in range(16):
                    group, b, e = k // 4, k // 2 % 2, k % 2
                    kt0 = 4 * group + 2 * e
                    if p_ == 0 and k in (2, 3):
                        fill_mix(FILL_MIX + 6 + k - 2)
                    if k == 0:
                        pe.wait_ge(*((swa_merged, 4) if p_ == 0 else (mixed_ready, 4)))
                    if k == 2:
                        pe.wait_ge(*((fill_lo, FILL_MIX + 6) if p_ == 0 else (out_scaled, TT)))
                    products(H_OUT + 16 * p_ + k, k,
                             lambda q, part, t: mix_view(kt0 + q, 1, part)[:, 0, t * P:(t + 1) * P],
                             banks[b], group == 0 and e == 0, group == 3 and e == 1,
                             wait=(fill_lo, FILL_MIX + kt0 // 2 + 1) if p_ == 0 else None,
                             early=last_half_tile0 if p_ == 1 and k == 15 else None)

            def up_half(i, k, bank):
                if k == 0 and not (isinstance(i, int) and i == 0):
                    pe.wait_ge(up_free, i)
                pe.wait_ge(lo_ready, 8 * i + (H_UP + k + 1))
                hi, lo = w_hi[:, k % HALF_SLOTS, :], w_lo[:, k % HALF_SLOTS, :]
                kt0 = k % 4 * 4
                for q in range(4):
                    kt = kt0 + q
                    if isinstance(i, int) and i == 0 and k < 4 and q % 2 == 0:
                        pe.wait_ge(fill_lo, FILL_H2 + kt // 2 + 1)
                    for f in range(2):
                        o = ps[:, bank + 2 * (k // 4) + f, :]
                        cols = slice(q * 2 * P + f * P, q * 2 * P + (f + 1) * P)
                        mm(o, hi[:, cols], xt[:, kt, :, :].rearrange("p l t -> p (l t)"),
                           start=kt == 0, stop=False, skip_group_check=True)
                        ins = mm(o[:, 0:SEQ], lo[:, cols], xt[:, kt, 0, :],
                                 start=False, stop=kt == KT - 1, skip_group_check=True)
                ins.then_inc(weights_used, 1)

            def fill_h2(b):
                pe.wait_ge(x2_ready, (2, 4, 4, 5)[b // 2])
                if b >= 4:
                    pe.wait_ge(x2_pool_ready, (2, 3)[b // 2 - 2])
                fill(FILL_H2 + b, lambda q, t: x2[:, t, (2 * b + q) * P:(2 * b + q + 1) * P])

            keep_warm(20)
            for b in range(4):
                fill_h2(b)
            for k in range(8):
                if k in (1, 2):
                    fill_h2(2 * k + 2)
                    fill_h2(2 * k + 3)
                up_half(0, k, 0)
            for k in range(8):
                if k == 2:
                    pe.wait_ge(diag_ready, 1)
                    for n in range(2):
                        for t in range(TT):
                            at = n * SEQ + t * P
                            ins = mm(ps[:, 6, at:at + P], ones[:], diag[:, t, :], start=True, stop=True)
                    ins.then_inc(rms_spread, 1)
                if k == 4:
                    pe.wait_ge(rms_copied, 1)
                up_half(1, k, 4)
            with pe.Fori(0, 10) as ii:
                for u in range(2):
                    for k in range(8):
                        up_half(2 * ii + 2 + u, k, 4 * u)

            def down(i, par, first, last):
                for k in range(8):
                    if k == 0:
                        pe.wait_ge(y_lo, i + 1)
                    if first and k in (0, 4):
                        pe.wait_ge(up_free, UP_GROUPS + k // 4)
                    e = k % 2
                    products(8 * i + (H_DOWN + k), k,
                             lambda q, part, t: y_split[:, par, 2 * e + q, part, t * P:(t + 1) * P],
                             2 * (k // 2), first and e == 0, last and e == 1,
                             early=last_half_tile0 if last and k == 7 else None)

            down(0, 0, True, False)
            with pe.Fori(0, 4) as ii:
                for u in range(2):
                    down(2 * ii + 1 + u, 1 - u, False, False)
            down(9, 1, False, False)
            down(10, 0, False, True)


def _tables():
    pos = np.arange(SEQ, dtype=np.float32)
    inv = (1.0 / (np.float32(10000.0) ** (np.arange(0, RET_DK, 2, dtype=np.float32) / RET_DK))).astype(np.float32)
    ang = (pos[:, None] * inv[None, :]).astype(np.float32)
    cs = np.stack([np.cos(ang), np.sin(ang)])
    cs = cs.reshape(2, TT, P, 64).transpose(2, 0, 1, 3)
    rope = np.ascontiguousarray(np.broadcast_to(cs[:, :, None], (P, 2, 2, TT, 64))).astype(np.float32)
    log_gamma = np.log(1.0 - 2.0 ** (-5.0 - np.arange(RET_HEADS, dtype=np.float64)))
    rel = np.arange(2 * P)[None, :] - np.arange(P)[:, None]
    decay = np.where(rel[:, None] >= 0, np.exp(log_gamma[None, :, None] * np.maximum(rel, 0)[:, None]), 0.0)
    decay = (decay * RET_DK ** -0.5).astype(np.float32)
    q, k = np.arange(P)[:, None], np.arange(P)[None, :]
    same = np.where(k <= q, 0.0, MASKED)
    before = np.where(k > q, 0.0, MASKED)
    band = np.concatenate([same, before, same], axis=1).astype(np.float32)
    return np.eye(P, dtype=np.float32), decay, rope, band


def _weight_stream(w_in, w_ret_o, w_swa_o, w_out, w_up, w_down):
    def blocks(w):
        k, n = w.shape
        return w.reshape(k // (4 * P), 4, P, n // NB, NB).transpose(3, 0, 2, 1, 4)

    order = [14, 0, 1, 2, 3, 4, 5, 6, 7, 12, 13, 8, 9, 10, 11, 15, 16, 17, 18, 19, 20, 21, 22]
    parts = [blocks(w_in)[order]]
    parts.append(np.concatenate([blocks(w_swa_o), blocks(w_ret_o)], axis=1))
    o = blocks(w_out)
    parts.append(o.reshape(2, 2, *o.shape[1:]).transpose(0, 2, 1, 3, 4, 5))
    up = w_up.reshape(2, 8, P, 2, UP_GROUPS, 256)
    parts.append(up.transpose(4, 3, 0, 2, 1, 5))
    down = w_down.reshape(DOWN_GROUPS, 4, P, 4, NB)
    parts.append(down.transpose(0, 3, 2, 1, 4))
    return np.concatenate([a.reshape(-1, P, CHUNK) for a in parts], axis=0)


def kernel(x, g_pre_mix, w_in, w_ret_o, w_swa_o, w_out, swa_sinks, g_post_mix,
           g_pre_ffn, w_up, conv_w, conv_b, w_down, g_post_ffn):
    import concourse.bacc as bacc
    from concourse.bass_utils import run_bass_kernel_spmd

    a = {k: np.asarray(v) for k, v in locals().items() if k not in ("bacc", "run_bass_kernel_spmd")}
    ident, decay, rope, band = _tables()
    arrays = {
        "weights": _weight_stream(a["w_in"][0], a["w_ret_o"][0], a["w_swa_o"][0], a["w_out"][0],
                                  a["w_up"][0], a["w_down"][0]),
        "x": a["x"][0],
        "ident_g_pre": np.concatenate([ident, a["g_pre_mix"][0].reshape(KT, P).T], axis=1),
        "g_ffn": np.ascontiguousarray(a["g_pre_ffn"][0].reshape(KT, P).T),
        "g_post_mix": np.ascontiguousarray(np.broadcast_to(a["g_post_mix"][0], (P, D_MODEL))),
        "g_post_ffn": np.ascontiguousarray(np.broadcast_to(a["g_post_ffn"][0], (P, D_MODEL))),
        "sinks": np.ascontiguousarray(np.broadcast_to(np.repeat(a["swa_sinks"][0], TT), (P, TT * SWA_HEADS))),
        "conv": np.ascontiguousarray(np.concatenate([a["conv_w"][0], a["conv_b"]], axis=0)
                                     .reshape(4, 2 * FF_TILES, P).transpose(2, 1, 0)),
        "decay": decay, "rope": rope, "band": band,
    }
    nc = bacc.Bacc("TRN2", target_bir_lowering=False, num_devices=1)
    args = {k: nc.dram_tensor(k, v.shape, mybir.dt.from_np(v.dtype), kind="ExternalInput").ap()
            for k, v in arrays.items()}
    out = nc.dram_tensor("out", (SEQ, D_MODEL), F32, kind="ExternalOutput").ap()
    build(nc, out=out, **args)
    r = run_bass_kernel_spmd(nc, [arrays], core_ids=[0])
    return r.results[0]["out"].reshape(1, SEQ, D_MODEL)
```

```python
from contextlib import ExitStack

import numpy as np

import concourse.bass as bass
from concourse import mybir

ALU = mybir.AluOpType
ACT = mybir.ActivationFunctionType
AX = mybir.AxisListType
F32 = mybir.dt.float32
F32R = mybir.dt.float32r
I32 = mybir.dt.int32

P = 128
D_MODEL = 2048
SEQ = 256
TT = SEQ // P
KT = D_MODEL // P
RET_HEADS, RET_DK, RET_DV = 8, 128, 256
SWA_HEADS, SWA_KV, SWA_DH, WINDOW = 16, 4, 64, 128
D_FF = 5632
EPS = 1e-6
NB = 512
CHUNK = 2048
HALF = CHUNK // 2
RAW_SLOTS = 4
HALF_SLOTS = 4

SK_AT = 0
SV_AT = SK_AT + SWA_KV * SWA_DH
RQ_AT = SV_AT + SWA_KV * SWA_DH
RK_AT = RQ_AT + RET_HEADS * RET_DK
RV_AT = RK_AT + RET_HEADS * RET_DK
SQ_AT = RV_AT + RET_HEADS * RET_DV
RG_AT = SQ_AT + SWA_HEADS * SWA_DH
GR_AT = RG_AT + RET_HEADS * RET_DV
GS_AT = GR_AT + D_MODEL
PROJ_W = GS_AT + D_MODEL
PROJ_BLOCKS = PROJ_W // NB

G_MERGE = PROJ_BLOCKS
G_OUT = G_MERGE + 6
G_UP = G_OUT + 4
UP_GROUPS = D_FF // 256
G_DOWN = G_UP + UP_GROUPS
DOWN_GROUPS = D_FF // (4 * P)
GROUPS = G_DOWN + DOWN_GROUPS
H_MERGE, H_OUT, H_UP, H_DOWN = (8 * g for g in (G_MERGE, G_OUT, G_UP, G_DOWN))
FF_TILES = D_FF // P

FILL_H = 0
FILL_SWA = FILL_H + KT // 2
FILL_RET = FILL_SWA + 4
FILL_MIX = FILL_RET + KT // 2
FILL_H2 = FILL_MIX + KT // 2

VECTOR_PIECES = (((0, 1024), (1024, 1024)), ((0, 256), (256, 512), (1536, 512)))
POOL_PIECES = ((768, 256), (1024, 256), (1280, 256))
VECTOR_X2 = ((0, 0, 256), (1, 0, 256), (0, 256, 256), (1, 256, 256), (0, 512, 512), (1, 512, 512),
             (1, 1536, 512))
POOL_X2 = ((0, 2), (1, 2), (0, 3))

MASKED = -3.0e38
RSQRT_MAGIC = float(0x5F3759DF - (3 << 23) - (1 << 31))


def fill_bank(f):
    return 4 + f % 4


def build(nc, weights, x, x_t, g_pre, g_ffn, g_post_mix, g_post_ffn, sinks, conv, ident, decay, rope, band, out):
    with ExitStack() as ctx:
        base = (nc.sbuf_base + 31) // 32 * 32

        def place(name, shape, dt, at):
            return nc.alloc_sbuf_tensor_at(name, shape, dt, offset=base + at)

        def sem(name):
            return ctx.enter_context(nc.semaphore(name))

        RAW_AT = 0
        HI_AT = RAW_AT + RAW_SLOTS * CHUNK * 4
        LO_AT = HI_AT + HALF_SLOTS * HALF * 4
        XT_AT = LO_AT + HALF_SLOTS * HALF * 4
        NAT0_AT = XT_AT + KT * 2 * SEQ * 4
        NAT1_AT = NAT0_AT + PROJ_W * 4
        X_AT = NAT1_AT + PROJ_W * 4
        SMALL_AT = X_AT + TT * D_MODEL * 4

        raw = place("raw", [P, RAW_SLOTS, CHUNK], F32, RAW_AT)
        w_hi = place("w_hi", [P, HALF_SLOTS, HALF], F32R, HI_AT)
        w_lo = place("w_lo", [P, HALF_SLOTS, HALF], F32R, LO_AT)
        xt = place("xt", [P, KT, 2, SEQ], F32R, XT_AT)
        nat = place("nat", [P, TT, PROJ_W], F32, NAT0_AT)
        x_t_in = place("x_t_in", [P, KT, SEQ], F32, NAT0_AT + GR_AT * 4)
        x_in = place("x_in", [P, TT, D_MODEL], F32, X_AT)

        decay_sb = place("decay_sb", [P, RET_HEADS, 2 * P], F32, X_AT)
        rope_sb = place("rope_sb", [P, 2, 2, TT, 64], F32, X_AT + 8192)
        qk_rot = place("qk_rot", [P, 2, TT, P], F32, X_AT + 10240)
        swa_qk = place("swa_qk", [P, 2, TT, P], F32, X_AT + 12288)
        swa_qk_t = place("swa_qk_t", [P, 2, SEQ], F32, X_AT + 14336)
        gs0, gs1 = NAT0_AT + GS_AT * 4, NAT1_AT + GS_AT * 4
        rot_tmp = place("rot_tmp", [P, 4, 2, TT, 64], F32, gs0)
        qk_t = place("qk_t", [P, 2, SEQ], F32, gs0 + 4096)
        ret_s = place("ret_s", [P, 3 * P], F32, gs0 + 6144)
        swa_p = place("swa_p", [P, 2, 3 * P], F32, gs1)
        swa_pt = place("swa_pt", [P, 2, 3 * P], F32, gs1 + 3072)
        band_sb = place("band_sb", [P, 3 * P], F32, gs1 + 6144)
        gate_t = place("gate_t", [P, 2, TT, NB], F32, NAT0_AT + RQ_AT * 4)
        swa_xt = place("swa_xt", [P, 8, 2, SEQ], F32R, X_AT)
        mix_t = place("mix_t", [P, 2, PROJ_W], F32R, NAT0_AT)
        gain_mix = place("gain_mix", [P, D_MODEL], F32, X_AT + D_MODEL * 4)
        x2 = place("x2", [P, TT, D_MODEL], F32, X_AT)
        y_t = place("y_t", [P, FF_TILES, SEQ], F32, NAT0_AT)
        y_split = place("y_split", [P, 2, 4, 2, SEQ], F32R, NAT1_AT)
        gain_ffn = place("gain_ffn", [P, D_MODEL], F32, NAT1_AT + 16384)
        up_lo = place("up_lo", [P, 4, SEQ], F32, NAT1_AT + 24576)
        up_pad = place("up_pad", [P, 4, SEQ + 2], F32, NAT1_AT + 28672)
        conv_o = place("conv_o", [P, 4, SEQ], F32, NAT1_AT + 32800)
        gelu_o = place("gelu_o", [P, 2, SEQ], F32, NAT1_AT + 36896)
        x2_rms_b = place("x2_rms_b", [P, 4, SEQ], F32, NAT1_AT + 38944)
        y_out = place("y_out", [P, TT, D_MODEL], F32, NAT1_AT + 24576)

        small = [SMALL_AT]

        def tile(name, shape):
            at, size = small[0], 4 * int(np.prod(shape[1:]))
            small[0] += (size + 31) // 32 * 32
            return place(name, shape, F32, at)

        ident_sb = tile("ident_sb", [P, P])
        g_pre_sb = tile("g_pre_sb", [P, KT])
        ones = tile("ones", [P, P])
        eps_sb = tile("eps_sb", [P, 1])
        load_table = tile("load_table", [P, 1])
        root = tile("root", [P, TT])
        g_ffn_sb = tile("g_ffn_sb", [P, KT])
        sinks_sb = tile("sinks_sb", [P, 2 * SWA_HEADS])
        conv_sb = tile("conv_sb", [P, 2 * FF_TILES, 4])
        x_ss = tile("x_ss", [P, TT, 4])
        x_rms = tile("x_rms", [P, TT])
        ret_ss = tile("ret_ss", [P, RET_HEADS, TT])
        ret_rms = tile("ret_rms", [P, RET_HEADS, TT])
        swa_mx = tile("swa_mx", [P, 4])
        swa_m = tile("swa_m", [P, 4])
        swa_neg = tile("swa_neg", [P, 4])
        swa_sd = tile("swa_sd", [P, 4])
        swa_sum = tile("swa_sum", [P, 4])
        swa_se = tile("swa_se", [P, 4])
        swa_den = tile("swa_den", [P, 4])
        swa_rden = tile("swa_rden", [P, 4])
        out_ss = tile("out_ss", [P, TT, 4])
        tot_ss = tile("tot_ss", [P, TT])
        out_rms = tile("out_rms", [P, TT])
        x2_ss = tile("x2_ss", [P, TT])
        x2_rms = tile("x2_rms", [P, TT])
        down_ss = tile("down_ss", [P, TT, 4])
        rs_v = tile("rs_v", [P, RET_HEADS * TT])
        rs_y = tile("rs_y", [P, TT])
        rs_t = tile("rs_t", [P, RET_HEADS * TT])
        diag = place("diag", [P, TT, P], F32, NAT0_AT + RG_AT * 4 - 2048)

        ps = ctx.enter_context(nc.psum_tensor("ps", [P, 8, NB], F32))

        x_t_landed = [sem(f"x_t_landed{i}") for i in range(8)]
        x_landed = [sem(f"x_landed{i}") for i in range(4)]
        quarter_landed = [sem(f"quarter_landed{i}") for i in range(2)]
        quarter_hi = sem("quarter_hi")
        quarter_lo = sem("quarter_lo")
        first_landed = [sem(f"first_landed{i}") for i in range(8)]
        small_landed = [sem(f"small_landed{i}") for i in range(5)]
        tables_landed = [sem(f"tables_landed{i}") for i in range(3)]
        x_again_landed = sem("x_again_landed")
        gain_mix_landed = sem("gain_mix_landed")
        gain_ffn_landed = sem("gain_ffn_landed")
        raw_landed = [sem(f"raw_landed{i}") for i in range(RAW_SLOTS)]
        hi_ready = sem("hi_ready")
        lo_ready = sem("lo_ready")
        weights_used = sem("weights_used")
        fill_done = sem("fill_done")
        fill_hi = sem("fill_hi")
        fill_lo = sem("fill_lo")
        order = sem("order")
        ones_ready = sem("ones_ready")
        x_squared = sem("x_squared")
        x_rms_ready = sem("x_rms_ready")
        z_free = sem("z_free")
        pool_order = sem("pool_order")
        qk_rotated = sem("qk_rotated")
        swa_staged = sem("swa_staged")
        ret_t_done = sem("ret_t_done")
        ret_t_copied = sem("ret_t_copied")
        ret_s_done = sem("ret_s_done")
        ret_masked = sem("ret_masked")
        ret_av_done = sem("ret_av_done")
        ret_out = sem("ret_out")
        swa_t_done = sem("swa_t_done")
        swa_t_copied = sem("swa_t_copied")
        swa_s_done = sem("swa_s_done")
        swa_max = sem("swa_max")
        swa_exp = sem("swa_exp")
        swa_pt_done = sem("swa_pt_done")
        swa_pt_copied = sem("swa_pt_copied")
        swa_av_done = sem("swa_av_done")
        swa_out = sem("swa_out")
        gate_tanh = sem("gate_tanh")
        ret_gated = sem("ret_gated")
        swa_gate_tanh = sem("swa_gate_tanh")
        swa_merged = sem("swa_merged")
        mixed_ready = sem("mixed_ready")
        out_tile0 = sem("out_tile0")
        last_used = sem("last_used")
        out_squared = sem("out_squared")
        x2_ready = sem("x2_ready")
        x2_scaled = sem("x2_scaled")
        x2_pool_ready = sem("x2_pool_ready")
        x2_squared = sem("x2_squared")
        diag_ready = sem("diag_ready")
        rms_spread = sem("rms_spread")
        rms_copied = sem("rms_copied")
        up_scaled = sem("up_scaled")
        up_low = sem("up_low")
        up_free = sem("up_free")
        tap0 = sem("tap0")
        taps = sem("taps")
        gelu = sem("gelu")
        y_ready = sem("y_ready")
        y_hi = sem("y_hi")
        y_lo = sem("y_lo")
        down_squared = sem("down_squared")
        out_scaled = sem("out_scaled")
        tot_ready = sem("tot_ready")
        root_ready = sem("root_ready")
        out_rms_ready = sem("out_rms_ready")
        piece_scaled = sem("piece_scaled")
        pool_result = sem("pool_result")
        pool_stored = sem("pool_stored")
        result = sem("result")
        stored = sem("stored")

        def pair(f):
            if f < FILL_SWA:
                return x_t_in[:, 2 * f:2 * f + 2, :]
            return ps[:, fill_bank(f), :].rearrange("p (q t) -> p q t", q=2)

        def fill_tile(f):
            return 2 * f if f < FILL_SWA else 2 * (f - FILL_H2)

        def mix_view(kt, n, part):
            at = (kt % 8) * 2 * SEQ
            v = mix_t[:, kt // 8, at:at + n * 2 * SEQ].rearrange("p (q l t) -> p q l t", q=n, l=2)
            return v[:, :, part, :]

        def fill_target(f, part):
            if FILL_MIX <= f < FILL_H2:
                return mix_view((f - FILL_MIX) * 2, 2, part)
            target, start = ((xt, FILL_H) if f < FILL_SWA else (swa_xt, FILL_SWA) if f < FILL_RET
                             else (xt, FILL_RET) if f < FILL_MIX else (xt, FILL_H2))
            b = (f - start) * 2
            return target[:, b:b + 2, part, :]

        def half_slot(k, part):
            return (w_hi, w_lo)[part][:, k % HALF_SLOTS, :]

        def last_slot(k, part):
            if k < HALF_SLOTS:
                return half_slot(k, part)
            at = 4 * (k - HALF_SLOTS) + 2 * part
            return xt[:, at:at + 2].rearrange("p q l t -> p (q l t)")

        block = ctx.enter_context(nc.Block())

        @block.sync
        def _(sp):
            wv = weights.rearrange("(g j) p n -> g j p n", j=RAW_SLOTS)
            for k in range(8):
                sp.dma_start(x_t_in[:, 2 * k:2 * k + 2, :], x_t[:, 2 * k:2 * k + 2, :])\
                    .then_inc(x_t_landed[k], 16)
                part = slice(k % 2 * HALF, (k % 2 + 1) * HALF)
                if k == 0:
                    for q in range(2):
                        cols = slice(q * NB, (q + 1) * NB)
                        sp.dma_start(raw[:, 0, cols], wv[0, 0][:, cols]).then_inc(quarter_landed[q], 16)
                else:
                    sp.dma_start(raw[:, k // 2, part], wv[0, k // 2][:, part]).then_inc(first_landed[k], 16)
            xv = x.rearrange("(t p) n -> p t n", p=P)
            for j in range(RAW_SLOTS):
                sp.wait_ge(lo_ready, 2 * j + 2)
                sp.dma_start(raw[:, j, :], wv[1, j]).then_inc(raw_landed[j], 16)
                cols = slice(j * NB, (j + 1) * NB)
                sp.dma_start(x_in[:, :, cols], xv[:, :, cols]).then_inc(x_landed[j], 16)
            with sp.Fori(2, GROUPS) as g:
                for j in range(RAW_SLOTS):
                    sp.wait_ge(lo_ready, 8 * g + 2 * j - 6)
                    sp.dma_start(raw[:, j, :], wv[bass.ds(g, 1), j].rearrange("a p n -> p (a n)"))\
                      .then_inc(raw_landed[j], 16)
            ov = out.rearrange("(t p) n -> p t n", p=P)
            pieces = [(t, c, n_cols) for t in range(TT) for c, n_cols in VECTOR_PIECES[t]]
            for n, (t, c, n_cols) in enumerate(pieces):
                sp.wait_ge(result, n + 1)
                sp.dma_start(ov[:, t, c:c + n_cols], y_out[:, t, c:c + n_cols]).then_inc(stored, 16)
            sp.wait_ge(stored, 16 * len(pieces))
            sp.wait_ge(pool_stored, 16 * len(POOL_PIECES))

        @block.gpsimd
        def _(pool):
            for k, (dst, src) in enumerate(((ident_sb, ident), (g_ffn_sb, g_ffn), (sinks_sb, sinks), (conv_sb, conv))):
                pool.dma_start(dst[:], src).then_inc(small_landed[k + 1], 16)
            pool.wait_ge(x_rms_ready, 1)
            for k, (dst, src) in enumerate(((decay_sb, decay), (rope_sb, rope), (band_sb, band))):
                pool.dma_start(dst[:], src).then_inc(tables_landed[k], 16)
            pool.wait_ge(tables_landed[1], 16)
            pool.wait_ge(z_free, 6)

            qk = nat[:, :, RQ_AT:RV_AT].rearrange("p t (w c) -> p w t c", w=2)
            step = [0]

            def rotate(s):
                lo = qk[:, :, :, bass.ds(RET_DK * s, 64)]
                hi = qk[:, :, :, bass.ds(RET_DK * s + 64, 64)]
                for n, (half, table) in enumerate(((lo, 0), (hi, 1), (lo, 1), (hi, 0))):
                    last = pool.tensor_tensor(rot_tmp[:, n], half, rope_sb[:, table], ALU.mult)
                last.then_inc(pool_order, 1)
                pool.wait_ge(pool_order, s + 1)
                pool.tensor_tensor(qk_rot[:, :, :, 0:64], rot_tmp[:, 0], rot_tmp[:, 1], ALU.subtract)
                pool.tensor_tensor(qk_rot[:, :, :, 64:128], rot_tmp[:, 2], rot_tmp[:, 3], ALU.add)\
                    .then_inc(qk_rotated, 1)

            def stage(s, kv, with_k):
                last = pool.tensor_copy(swa_qk[:, 0], nat[:, :, bass.ds(SQ_AT + P * s, P)])
                for a in range(2 * with_k):
                    last = pool.tensor_copy(swa_qk[:, 1, :, 64 * a:64 * a + 64],
                                            nat[:, :, bass.ds(SK_AT + SWA_DH * kv, SWA_DH)])
                last.then_inc(swa_staged, 1)

            def heads(i, first):
                for u in range(2):
                    s = 2 * i + u
                    if not (first and u == 0):
                        pool.wait_ge(ret_t_done, s)
                        pool.wait_ge(qk_rotated, s)
                    rotate(s)
                    if first:
                        pool.wait_ge(z_free, 11 + u)
                    if not (first and u == 0):
                        pool.wait_ge(swa_t_done, s)
                    stage(s, i, u == 0)

            heads(0, True)
            with pool.Fori(1, 4) as i:
                heads(i, False)
            pool.wait_ge(ret_gated, 4)
            pool.dma_start(nat[:, :, RG_AT:GR_AT], x.rearrange("(t p) n -> p t n", p=P))\
                .then_inc(x_again_landed, 16)
            pool.wait_ge(weights_used, H_OUT)
            pool.dma_start(gain_mix[:], g_post_mix).then_inc(gain_mix_landed, 16)
            pool.wait_ge(x_again_landed, 16)
            for n, (t, c) in enumerate(POOL_X2):
                cols = slice(c * NB, (c + 1) * NB)
                pool.wait_ge(x2_scaled, n + 1)
                pool.tensor_tensor(x2[:, t, cols], nat[:, t, GS_AT:PROJ_W][:, cols],
                                   nat[:, t, RG_AT:GR_AT][:, cols], ALU.add).then_inc(x2_pool_ready, 1)
            pool.wait_ge(fill_done, FILL_H2 + 8 - FILL_SWA)
            pool.dma_start(gain_ffn[:], g_post_ffn).then_inc(gain_ffn_landed, 16)

            pool.wait_ge(rms_copied, 1)

            def scale_group():
                pool.tensor_tensor(up_pad[:, :, 2:SEQ + 2], up_lo[:], x2_rms_b[:], ALU.mult)\
                    .then_inc(up_scaled, 1)

            pool.wait_ge(up_free, 2)
            scale_group()
            with pool.Fori(1, UP_GROUPS) as i:
                pool.wait_ge(up_free, i + 2)
                pool.wait_ge(taps, i)
                scale_group()

            for n, (c, n_cols) in enumerate(POOL_PIECES):
                cols = slice(c, c + n_cols)
                pool.wait_ge(piece_scaled, n + 1)
                pool.tensor_tensor(y_out[:, 1, cols], y_out[:, 1, cols], x2[:, 1, cols], ALU.add)\
                    .then_inc(pool_result, 1)

        @block.scalar
        def _(act):
            def split_hi(g, k, slot=half_slot):
                if isinstance(g, int) and g == 0:
                    act.wait_ge(first_landed[k], 16)
                elif k % 2 == 0:
                    act.wait_ge(raw_landed[k // 2], 16 * g)
                if not (isinstance(g, int) and (8 * g + k < HALF_SLOTS or slot is last_slot and k >= HALF_SLOTS)):
                    act.wait_ge(weights_used, 8 * g + k - (HALF_SLOTS - 1))
                nc.scalar.activation(slot(k, 0),
                                     raw[:, k // 2, (k % 2) * HALF:(k % 2 + 1) * HALF],
                                     ACT.Copy).then_inc(hi_ready, 1)

            def high(f, scale=1.0, gain=None):
                if f < FILL_SWA:
                    act.wait_ge(x_t_landed[f], 16)
                else:
                    act.wait_ge(fill_done, f - FILL_SWA + 1)
                if gain is None:
                    nc.scalar.activation(fill_target(f, 0), pair(f), ACT.Copy, scale=scale)\
                        .then_inc(fill_hi, 1)
                    return
                kt = fill_tile(f)
                for q in range(2):
                    last = nc.scalar.activation(fill_target(f, 0)[:, q, :], pair(f)[:, q, :], ACT.Copy,
                                                scale=gain[:, kt + q:kt + q + 1])
                last.then_inc(fill_hi, 1)

            def evict(m, bank):
                act.wait_ge(weights_used, 8 * m + 8)
                for t in range(TT):
                    last = nc.scalar.activation(nat[:, t, bass.ds(NB * m, NB)], ps[:, bank + t, :],
                                                ACT.Copy, scale=x_rms[:, t:t + 1])
                last.then_inc(z_free, 1)

            act.dma_start(g_pre_sb[:], g_pre).then_inc(small_landed[0], 16)
            act.wait_ge(ones_ready, 1)
            nc.scalar.activation(swa_m[:], ones[:, 0:4], ACT.Copy).then_inc(z_free, 1)

            act.wait_ge(small_landed[0], 16)
            high(FILL_H, gain=g_pre_sb)
            for q in range(2):
                cols = slice(q * NB, (q + 1) * NB)
                act.wait_ge(quarter_landed[q], 16)
                nc.scalar.activation(w_hi[:, 0, cols], raw[:, 0, cols], ACT.Copy)\
                    .then_inc(hi_ready if q else quarter_hi, 1)
            for k in range(1, 8):
                high(FILL_H + k, gain=g_pre_sb)
                split_hi(0, k)

            for k in range(8):
                split_hi(1, k)
                if k % 2 == 1:
                    cols = slice(k // 2 * NB, (k // 2 + 1) * NB)
                    act.wait_ge(x_landed[k // 2], 16)
                    nc.scalar.activation(nat[:, 1, GS_AT:PROJ_W][:, cols], x_in[:, 1, cols], ACT.Square,
                                         accum_out=x_ss[:, 1, k // 2:k // 2 + 1]).then_inc(x_squared, 1)
            split_hi(2, 0)
            act.wait_ge(x_rms_ready, 1)
            evict(0, 0)

            for k in range(1, 8):
                split_hi(2, k)
                if k == 3:
                    evict(1, 2)
            with act.Fori(0, 4) as i:
                for u in range(2):
                    for k in range(8):
                        split_hi(2 * i + 3 + u, k)
                        if k == 3:
                            evict(2 * i + 2 + u, 2 * u)

            with act.Fori(0, 4) as i:
                for u in range(2):
                    s = 2 * i + u
                    for k in range(8):
                        split_hi(2 * i + 11 + u, k)
                        if k == 3:
                            evict(2 * i + 10 + u, 2 * u)
                            act.wait_ge(ret_t_done, s + 1)
                            nc.scalar.activation(qk_t[:], ps[:, 4, :].rearrange("p (w t) -> p w t", w=2),
                                                 ACT.Copy).then_inc(ret_t_copied, 1)
                            act.wait_ge(swa_t_done, s + 1)
                            new = SEQ * (2 - u)
                            nc.scalar.activation(swa_qk_t[:].rearrange("p w t -> p (w t)")[:, 0:new],
                                                 ps[:, 5, 0:new], ACT.Copy).then_inc(swa_t_copied, 1)
                        if k == 4:
                            act.wait_ge(swa_max, s + 1)
                            for a in range(2):
                                for t, cols in ((0, slice(0, P)), (1, slice(P, 3 * P))):
                                    j = 2 * a + t
                                    nc.scalar.activation(swa_p[:, a, cols], swa_p[:, a, cols], ACT.Exp,
                                                         bias=swa_neg[:, j:j + 1], scale=SWA_DH ** -0.5,
                                                         accum_out=swa_sum[:, j:j + 1])
                            nc.scalar.activation(swa_se[:], swa_sd[:], ACT.Exp).then_inc(swa_exp, 1)
                        if k == 6:
                            act.wait_ge(ret_av_done, s + 1)
                            for t in range(TT):
                                nc.scalar.activation(qk_t[:, t, :], ps[:, 4, t * RET_DV:(t + 1) * RET_DV],
                                                     ACT.Square, accum_out=ret_ss[:, bass.ds(s, 1), t])
                            nc.scalar.activation(nat[:, :, bass.ds(RV_AT + RET_DV * s, RET_DV)],
                                                 ps[:, 4, :].rearrange("p (t v) -> p t v", t=TT),
                                                 ACT.Copy).then_inc(ret_out, 1)
                        if k == 7:
                            act.wait_ge(swa_pt_done, s + 1)
                            for a in range(2):
                                last = nc.scalar.activation(swa_pt[:, a, :], ps[:, 7 - 2 * a, 0:3 * P], ACT.Copy)
                            last.then_inc(swa_pt_copied, 1)

            for j in range(4):
                for k in range(8):
                    split_hi(19 + j, k)
                    if k == 3:
                        evict(18 + j, 2 * (j % 2))
                        high(FILL_SWA + j)
                    if k == 4:
                        act.wait_ge(z_free, j + 17)
                        nc.scalar.activation(gate_t[:, j % 2], nat[:, :, RG_AT + NB * j:RG_AT + NB * (j + 1)],
                                             ACT.Tanh, scale=0.5).then_inc(gate_tanh, 1)
                    if k == 5:
                        gr = nat[:, :, GR_AT + NB * j:GR_AT + NB * (j + 1)]
                        nc.scalar.activation(gr, gr, ACT.Tanh, scale=0.5)

            for n in range(4):
                for k in range(12):
                    split_hi(G_MERGE + (12 * n + k) // 8, (12 * n + k) % 8)
                    if n == 0:
                        if k == 3:
                            evict(PROJ_BLOCKS - 1, 0)
                            act.wait_ge(weights_used, H_MERGE)
                        if 3 <= k <= 6:
                            high(FILL_RET + 2 * (k - 3))
                            high(FILL_RET + 2 * (k - 3) + 1)
                    elif k in (5, 6):
                        high(FILL_MIX + 2 * (n - 1) + k - 5, scale=0.5)
                    if k == 6:
                        act.wait_ge(z_free, PROJ_BLOCKS + 1)
                        gs = nat[:, :, GS_AT + NB * n:GS_AT + NB * (n + 1)]
                        nc.scalar.activation(gs, gs, ACT.Tanh, scale=0.5).then_inc(swa_gate_tanh, 1)

            def take_root(count, t=0, n=TT):
                act.wait_ge(tot_ready, count)
                nc.scalar.activation(root[:, t:t + n], tot_ss[:, t:t + n], ACT.Sqrt, bias=eps_sb[:], scale=1.0 / D_MODEL)\
                    .then_inc(root_ready, 1)

            def squares(t, nb, bank):
                nc.scalar.activation(nat[:, t, GR_AT + NB * nb:GR_AT + NB * (nb + 1)], ps[:, bank + t, :],
                                     ACT.Square, accum_out=out_ss[:, t, nb:nb + 1]).then_inc(out_squared, 1)

            for p_ in range(2):
                for k in range(16):
                    split_hi(G_OUT + 2 * p_ + k // 8, k % 8)
                    if p_ == 0 and k in (5, 6):
                        high(FILL_MIX + 6 + k - 5, scale=0.5)
                    if p_ == 1 and k == 1:
                        nc.scalar.activation(load_table[:], eps_sb[:], ACT.Sqrt)
                    if p_ == 1 and k == 3:
                        act.wait_ge(weights_used, H_OUT + 16)
                        for nb, bank in ((0, 2), (1, 4)):
                            for t in range(TT):
                                squares(t, nb, bank)

            for k in range(2):
                split_hi(G_UP, k)
            act.wait_ge(weights_used, H_UP - 2)
            for t in range(TT):
                squares(t, 2, 0)
            split_hi(G_UP, 2)
            act.wait_ge(out_tile0, 1)
            squares(0, 3, 2)
            act.wait_ge(weights_used, H_UP)
            squares(1, 3, 2)
            take_root(1)
            split_hi(G_UP, 3)
            act.wait_ge(out_rms_ready, 1)
            for t, c in POOL_X2:
                part = nat[:, t, GS_AT + NB * c:GS_AT + NB * (c + 1)]
                nc.scalar.activation(part, part, ACT.Copy, scale=out_rms[:, t:t + 1]).then_inc(x2_scaled, 1)
            act.wait_ge(small_landed[2], 16)
            for k in range(8):
                high(FILL_H2 + k, gain=g_ffn_sb)
                if k in (5, 7):
                    split_hi(G_UP, 4 + k // 7)
            act.wait_ge(x2_ready, len(VECTOR_X2))
            act.wait_ge(x2_pool_ready, len(POOL_X2))
            for t in range(TT):
                nc.scalar.activation(nat[:, t, GS_AT:PROJ_W], x2[:, t, :], ACT.Square,
                                     accum_out=x2_ss[:, t:t + 1]).then_inc(x2_squared, 1)
            for k in (6, 7):
                split_hi(G_UP, k)

            def up_tile(i, f):
                return 2 * i + f if f < 2 else FF_TILES + 2 * i + f - 2

            def up_group_out(i, k, bank):
                if k == 3:
                    act.wait_ge(weights_used, H_UP + 8 * i + 8)
                    nc.scalar.activation(up_lo[:], ps[:, bank:bank + 4, SEQ:2 * SEQ], ACT.Copy)\
                        .then_inc(up_low, 1)
                if k == 6:
                    act.wait_ge(up_scaled, i + 1)
                    for f in range(4):
                        c = conv_sb[:, bass.ds(up_tile(i, f), 1), :]
                        last = nc.scalar.activation(conv_o[:, f, :], up_pad[:, f, 0:SEQ], ACT.Identity,
                                                    scale=c[:, 0, 0:1], bias=c[:, 0, 3:4])
                    last.then_inc(tap0, 1)
                if k == 7:
                    act.wait_ge(taps, i + 1)
                    nc.scalar.activation(gelu_o[:], conv_o[:, 2:4, :], ACT.Gelu_apprx_tanh)\
                        .then_inc(gelu, 1)

            act.wait_ge(small_landed[4], 16)
            for k in range(8):
                split_hi(G_UP + 1, k)
                if k == 5:
                    act.wait_ge(rms_spread, 1)
                    for n in range(2):
                        last = nc.scalar.activation(x2_rms_b[:, 2 * n:2 * n + 2, :],
                                                    ps[:, 6, :].rearrange("p (f t) -> p f t", f=2), ACT.Copy)
                    last.then_inc(rms_copied, 1)
                up_group_out(0, k, 0)
            with act.Fori(0, 10) as ii:
                for u in range(2):
                    for k in range(8):
                        split_hi(2 * ii + G_UP + 2 + u, k)
                        up_group_out(2 * ii + 1 + u, k, 4 * (1 - u))

            def stage_hi(i, par):
                nc.scalar.activation(y_split[:, par, :, 0, :], y_t[:, bass.ds(4 * i, 4), :], ACT.Copy)\
                    .then_inc(y_hi, 1)

            act.wait_ge(y_ready, 2)
            stage_hi(0, 0)
            for k in range(8):
                split_hi(G_DOWN, k)
                up_group_out(21, k, 4)
            act.wait_ge(y_ready, UP_GROUPS)
            stage_hi(1, 1)
            with act.Fori(0, 4) as ii:
                for u in range(2):
                    i = 2 * ii + 1 + u
                    for k in range(8):
                        split_hi(2 * ii + G_DOWN + 1 + u, k)
                        if k == 4:
                            stage_hi(i + 1, u)
            for k in range(8):
                split_hi(G_DOWN + 9, k)
                if k == 4:
                    stage_hi(10, 0)
                if k == 6:
                    nc.scalar.activation(load_table[:], root[:, 0:1], ACT.Sqrt)
            for k in range(8):
                split_hi(G_DOWN + 10, k, last_slot)

            for t in range(TT):
                for nb in range(4):
                    act.wait_ge(last_used, 8 * t + 2 * nb + 2)
                    nc.scalar.activation(raw[:, nb, t * NB:(t + 1) * NB], ps[:, 2 * nb + t, :], ACT.Square,
                                         accum_out=down_ss[:, t, nb:nb + 1]).then_inc(down_squared, 1)
                take_root(2 + t, t, 1)
            act.wait_ge(out_rms_ready, 3)
            for c, n_cols in POOL_PIECES:
                cols = slice(c, c + n_cols)
                nc.scalar.activation(y_out[:, 1, cols], y_out[:, 1, cols], ACT.Copy,
                                     scale=out_rms[:, 1:2]).then_inc(piece_scaled, 1)
            for n, (c, n_cols) in enumerate(POOL_PIECES):
                cols = slice(c, c + n_cols)
                act.wait_ge(pool_result, n + 1)
                act.dma_start(out.rearrange("(t p) n -> p t n", p=P)[:, 1, cols], y_out[:, 1, cols])\
                    .then_inc(pool_stored, 16)

        @block.vector
        def _(dve):
            chain = [0]

            def link(ins):
                ins.then_inc(order, 1)
                chain[0] = chain[0] + 1
                dve.wait_ge(order, chain[0])

            def split_lo(g, k, slot=half_slot):
                dve.wait_ge(hi_ready, 8 * g + k + 1)
                nc.vector.tensor_tensor(slot(k, 1),
                                        raw[:, k // 2, (k % 2) * HALF:(k % 2 + 1) * HALF],
                                        slot(k, 0).bitcast(F32), ALU.subtract)\
                    .then_inc(lo_ready, 1)

            def low(f, scale=1.0, gain=None):
                dve.wait_ge(fill_hi, f + 1)
                hi = fill_target(f, 0).bitcast(F32)
                if gain is None:
                    nc.vector.scalar_tensor_tensor(out=fill_target(f, 1), in0=pair(f), scalar=scale, in1=hi,
                                                   op0=ALU.mult, op1=ALU.subtract).then_inc(fill_lo, 1)
                    return
                kt = fill_tile(f)
                for q in range(2):
                    last = nc.vector.scalar_tensor_tensor(
                        out=fill_target(f, 1)[:, q, :], in0=pair(f)[:, q, :],
                        scalar=gain[:, kt + q:kt + q + 1], in1=hi[:, q, :],
                        op0=ALU.mult, op1=ALU.subtract)
                last.then_inc(fill_lo, 1)

            def rsqrt(y, ss, n, width, signal=None):
                v, t = rs_v[:, 0:n], rs_t[:, 0:n]
                link(nc.vector.tensor_scalar(v, ss, 1.0 / width, EPS, ALU.mult, ALU.add))
                link(nc.vector.tensor_scalar(y.bitcast(I32), v.bitcast(I32), -0.5, RSQRT_MAGIC,
                                             ALU.mult, ALU.add))
                for n_, scale in enumerate((64.0, 16.0, 4.0)):
                    link(nc.vector.scalar_tensor_tensor(out=t, in0=y, scalar=scale, in1=y,
                                                        op0=ALU.mult, op1=ALU.mult))
                    link(nc.vector.tensor_tensor(t, t, v, ALU.mult))
                    last = nc.vector.scalar_tensor_tensor(out=y, in0=t, scalar=-3.0, in1=y,
                                                          op0=ALU.add, op1=ALU.mult)
                    if n_ < 2 or signal is None:
                        link(last)
                    else:
                        last.then_inc(signal[0], 1)
                        dve.wait_ge(*signal)

            def rms_from_root(ss, count, at=0, n=TT):
                tiles = slice(at, at + n)
                v, t, y, tot = rs_v[:, tiles], rs_t[:, tiles], rs_y[:, tiles], tot_ss[:, tiles]
                nc.vector.tensor_reduce(tot, ss[:, tiles], AX.X, ALU.add).then_inc(tot_ready, 1)
                dve.wait_ge(tot_ready, count)
                nc.vector.tensor_scalar(v, tot, 1.0 / D_MODEL, EPS, ALU.mult, ALU.add)
                dve.wait_ge(root_ready, count)
                link(nc.vector.reciprocal(y, root[:, tiles]))
                link(nc.vector.scalar_tensor_tensor(out=t, in0=y, scalar=-0.5, in1=y,
                                                    op0=ALU.mult, op1=ALU.mult))
                link(nc.vector.tensor_tensor(t, t, v, ALU.mult))
                nc.vector.scalar_tensor_tensor(out=out_rms[:, tiles], in0=t, scalar=1.5, in1=y,
                                               op0=ALU.add, op1=ALU.mult).then_inc(out_rms_ready, 1)
                dve.wait_ge(out_rms_ready, count)

            nc.vector.memset(eps_sb[:], EPS)
            nc.vector.memset(ones[:], 1.0).then_inc(ones_ready, 1)
            dve.wait_ge(small_landed[0], 16)
            low(FILL_H, gain=g_pre_sb)
            for q in range(2):
                cols = slice(q * NB, (q + 1) * NB)
                dve.wait_ge(*((hi_ready, 1) if q else (quarter_hi, 1)))
                nc.vector.tensor_tensor(w_lo[:, 0, cols], raw[:, 0, cols], w_hi[:, 0, cols].bitcast(F32),
                                        ALU.subtract).then_inc(lo_ready if q else quarter_lo, 1)
            for k in range(1, 8):
                low(FILL_H + k, gain=g_pre_sb)
                split_lo(0, k)

            for k in range(8):
                split_lo(1, k)
                if k % 2 == 1:
                    cols = slice(k // 2 * NB, (k // 2 + 1) * NB)
                    dve.wait_ge(x_landed[k // 2], 16)
                    last = nc.vector.tensor_tensor_reduce(
                        out=nat[:, 0, GS_AT:PROJ_W][:, cols], in0=x_in[:, 0, cols], in1=x_in[:, 0, cols],
                        scale=1.0, scalar=0.0, op0=ALU.mult, op1=ALU.add,
                        accum_out=x_ss[:, 0, k // 2:k // 2 + 1])
            link(last)
            dve.wait_ge(x_squared, 4)
            link(nc.vector.tensor_reduce(tot_ss[:], x_ss[:], AX.X, ALU.add))
            rsqrt(x_rms[:], tot_ss[:], TT, D_MODEL, signal=(x_rms_ready, 1))
            with dve.Fori(2, 11) as g:
                for k in range(8):
                    split_lo(g, k)

            dve.wait_ge(tables_landed[0], 16)
            dve.wait_ge(tables_landed[2], 16)
            dve.wait_ge(small_landed[3], 16)
            LINKS = 5
            start = chain[0]
            with dve.Fori(0, 4) as i:
                for u in range(2):
                    s = 2 * i + u
                    chain[0] = 2 * LINKS * i + (start + LINKS * u)
                    for k in range(8):
                        split_lo(2 * i + 11 + u, k)
                        if k == 3:
                            dve.wait_ge(ret_s_done, s + 1)
                            nc.vector.tensor_tensor(ret_s[:, 0:2 * P].rearrange("p (a n) -> p a n", a=1),
                                                    ps[:, 6:7, 0:2 * P],
                                                    decay_sb[:, bass.ds(s, 1), :], ALU.mult)
                            nc.vector.tensor_tensor(ret_s[:, 2 * P:3 * P].rearrange("p (a n) -> p a n", a=1),
                                                    ps[:, 6:7, 2 * P:3 * P],
                                                    decay_sb[:, bass.ds(s, 1), 0:P], ALU.mult)\
                                .then_inc(ret_masked, 1)
                            dve.wait_ge(swa_s_done, s + 1)
                            nc.vector.tensor_tensor(swa_p[:, 0, :], ps[:, 7, 0:3 * P], band_sb[:], ALU.add)
                            link(nc.vector.tensor_tensor(swa_p[:, 1, :], ps[:, 5, 0:3 * P], band_sb[:], ALU.add))
                            mx = swa_mx[:].rearrange("p (a t) -> p a t", a=2)
                            nc.vector.tensor_reduce(mx[:, :, 0], swa_p[:, :, 0:P], AX.X, ALU.max)
                            link(nc.vector.tensor_reduce(mx[:, :, 1], swa_p[:, :, P:3 * P], AX.X, ALU.max))
                            sink = sinks_sb[:, bass.ds(4 * s, 4)]
                            link(nc.vector.scalar_tensor_tensor(
                                out=swa_m[:], in0=swa_mx[:], scalar=SWA_DH ** -0.5, in1=sink,
                                op0=ALU.mult, op1=ALU.max))
                            nc.vector.tensor_scalar(swa_neg[:], swa_m[:], -1.0, None, ALU.mult)
                            nc.vector.tensor_tensor(swa_sd[:], sink, swa_m[:], ALU.subtract)\
                                .then_inc(swa_max, 1)
                        if k == 5:
                            dve.wait_ge(swa_exp, s + 1)
                            link(nc.vector.tensor_tensor(swa_den[:], swa_sum[:], swa_se[:], ALU.add))
                            link(nc.vector.reciprocal(swa_rden[:], swa_den[:]))
                    dve.wait_ge(swa_av_done, s + 1)
                    for a in range(2):
                        for t in range(TT):
                            j = 2 * a + t
                            last = nc.vector.tensor_scalar(
                                nat[:, t, bass.ds(SQ_AT + P * s + SWA_DH * a, SWA_DH)],
                                ps[:, 6, SWA_DH * j:SWA_DH * (j + 1)], swa_rden[:, j:j + 1], None, ALU.mult)
                    last.then_inc(swa_out, 1)
            chain[0] = start + 8 * LINKS

            dve.wait_ge(ret_out, RET_HEADS)
            rr = ret_rms[:].rearrange("p h t -> p (h t)")
            rsqrt(rr, ret_ss[:].rearrange("p h t -> p (h t)"), RET_HEADS * TT, RET_DV)
            link(nc.vector.tensor_scalar(rr, rr, 0.5, None, ALU.mult))
            for j in range(4):
                for k in range(8):
                    split_lo(19 + j, k)
                    if k == 3:
                        low(FILL_SWA + j)
                    if k == 4:
                        dve.wait_ge(gate_tanh, j + 1)
                        rg = nat[:, :, RG_AT + NB * j:RG_AT + NB * (j + 1)]
                        link(nc.vector.scalar_tensor_tensor(out=rg, in0=gate_t[:, j % 2], scalar=1.0, in1=rg,
                                                            op0=ALU.add, op1=ALU.mult))
                    if k == 6:
                        for a in range(2):
                            for t in range(TT):
                                at = NB * j + RET_DV * a
                                ret = nat[:, t, RV_AT + at:RV_AT + at + RET_DV]
                                last = nc.vector.scalar_tensor_tensor(
                                    out=ret, in0=ret, scalar=ret_rms[:, 2 * j + a, t:t + 1],
                                    in1=nat[:, t, RG_AT + at:RG_AT + at + RET_DV],
                                    op0=ALU.mult, op1=ALU.mult)
                        last.then_inc(ret_gated, 1)

            def gates(n):
                return (nat[:, :, GR_AT + NB * n:GR_AT + NB * (n + 1)],
                        nat[:, :, GS_AT + NB * n:GS_AT + NB * (n + 1)])

            def merge_swa(n):
                dve.wait_ge(weights_used, H_MERGE + 12 * n + 4)
                dve.wait_ge(swa_gate_tanh, n + 1)
                gs = gates(n)[1]
                nc.vector.scalar_tensor_tensor(out=gs, in0=gs, scalar=1.0, in1=ps[:, 2:4, :],
                                               op0=ALU.add, op1=ALU.mult).then_inc(swa_merged, 1)

            def merge_ret(n):
                dve.wait_ge(weights_used, H_MERGE + 12 * n + 12)
                gr, gs = gates(n)
                link(nc.vector.scalar_tensor_tensor(out=gr, in0=gr, scalar=1.0, in1=ps[:, 0:2, :],
                                                    op0=ALU.add, op1=ALU.mult))
                nc.vector.tensor_tensor(gr, gr, gs, ALU.add).then_inc(mixed_ready, 1)

            for n in range(4):
                for k in range(12):
                    split_lo(G_MERGE + (12 * n + k) // 8, (12 * n + k) % 8)
                    if n == 0:
                        if 3 <= k <= 6:
                            low(FILL_RET + 2 * (k - 3))
                            low(FILL_RET + 2 * (k - 3) + 1)
                    else:
                        if k == 3:
                            merge_ret(n - 1)
                        if k in (5, 6):
                            low(FILL_MIX + 2 * (n - 1) + k - 5, scale=0.5)
                    if k == 8:
                        merge_swa(n)

            def scale_out(t, nb, bank):
                dve.wait_ge(out_squared, 2 * nb + t + 1)
                return nc.vector.tensor_tensor(nat[:, t, GS_AT + NB * nb:GS_AT + NB * (nb + 1)],
                                               ps[:, bank + t, :], gain_mix[:, NB * nb:NB * (nb + 1)],
                                               ALU.mult)

            for p_ in range(2):
                for k in range(16):
                    split_lo(G_OUT + 2 * p_ + k // 8, k % 8)
                    if p_ == 0:
                        if k == 3:
                            merge_ret(3)
                        if k in (5, 6):
                            low(FILL_MIX + 6 + k - 5, scale=0.5)
                    elif k == 3:
                        dve.wait_ge(gain_mix_landed, 16)
                        for nb, bank in ((0, 2), (1, 4)):
                            for t in range(TT):
                                scale_out(t, nb, bank).then_inc(out_scaled, 1)

            for k in range(2):
                split_lo(G_UP, k)
            for t in range(TT):
                scale_out(t, 2, 0)
            split_lo(G_UP, 2)
            link(scale_out(0, 3, 2))
            dve.wait_ge(out_squared, 4 * TT)
            rms_from_root(out_ss, 1)
            dve.wait_ge(x_again_landed, 16)

            def residual(t, c, n_cols):
                cols = slice(c, c + n_cols)
                nc.vector.scalar_tensor_tensor(out=x2[:, t, cols], in0=nat[:, t, GS_AT:PROJ_W][:, cols],
                                               scalar=out_rms[:, t:t + 1],
                                               in1=nat[:, t, RG_AT:GR_AT][:, cols],
                                               op0=ALU.mult, op1=ALU.add).then_inc(x2_ready, 1)

            for piece in VECTOR_X2[:-1]:
                residual(*piece)
            for c in range(4):
                low(FILL_H2 + 2 * c, gain=g_ffn_sb)
                low(FILL_H2 + 2 * c + 1, gain=g_ffn_sb)
                if c == 1:
                    link(scale_out(1, 3, 2))
                    residual(*VECTOR_X2[-1])
                if c > 0:
                    split_lo(G_UP, 2 + c)
            nc.vector.memset(up_pad[:, :, 0:2], 0.0).then_inc(up_free, 1)
            dve.wait_ge(x2_squared, 2)
            rsqrt(x2_rms[:], x2_ss[:], TT, D_MODEL)
            for t in range(TT):
                last = nc.vector.tensor_scalar(diag[:, t, :], ident_sb[:], x2_rms[:, t:t + 1], None, ALU.mult)
            last.then_inc(diag_ready, 1)
            for k in (6, 7):
                split_lo(G_UP, k)

            def up_tile(i, f):
                return 2 * i + f if f < 2 else FF_TILES + 2 * i + f - 2

            UP_LINKS = 1

            def up_group_out(i, k, bank):
                if k == 3:
                    dve.wait_ge(up_low, i + 1)
                    nc.vector.tensor_tensor(up_lo[:], ps[:, bank:bank + 4, 0:SEQ], up_lo[:],
                                            ALU.add).then_inc(up_free, 1)
                if k == 6:
                    dve.wait_ge(tap0, i + 1)
                    for tap in (1, 2):
                        for f in range(4):
                            last = nc.vector.scalar_tensor_tensor(
                                out=conv_o[:, f, :], in0=up_pad[:, f, tap:tap + SEQ],
                                scalar=conv_sb[:, bass.ds(up_tile(i, f), 1), tap], in1=conv_o[:, f, :],
                                op0=ALU.mult, op1=ALU.add)
                        if tap == 1:
                            link(last)
                    last.then_inc(taps, 1)
                if k == 7:
                    dve.wait_ge(gelu, i + 1)
                    nc.vector.tensor_tensor(y_t[:, bass.ds(2 * i, 2), :], conv_o[:, 0:2, :], gelu_o[:],
                                            ALU.mult).then_inc(y_ready, 1)

            start = chain[0]
            for k in range(8):
                split_lo(G_UP + 1, k)
                up_group_out(0, k, 0)
            with dve.Fori(0, 10) as ii:
                for u in range(2):
                    chain[0] = 2 * UP_LINKS * ii + (start + UP_LINKS * (1 + u))
                    for k in range(8):
                        split_lo(2 * ii + G_UP + 2 + u, k)
                        up_group_out(2 * ii + 1 + u, k, 4 * (1 - u))
            chain[0] = start + 21 * UP_LINKS

            def stage_lo(i, par):
                dve.wait_ge(y_hi, i + 1)
                nc.vector.tensor_tensor(y_split[:, par, :, 1, :], y_t[:, bass.ds(4 * i, 4), :],
                                        y_split[:, par, :, 0, :].bitcast(F32), ALU.subtract)\
                    .then_inc(y_lo, 1)

            stage_lo(0, 0)
            for k in range(8):
                split_lo(G_DOWN, k)
                up_group_out(21, k, 4)
            stage_lo(1, 1)
            with dve.Fori(0, 4) as ii:
                for u in range(2):
                    for k in range(8):
                        split_lo(2 * ii + G_DOWN + 1 + u, k)
                        if k == 4:
                            stage_lo(2 * ii + 2 + u, u)
            for k in range(8):
                split_lo(G_DOWN + 9, k)
                if k == 4:
                    stage_lo(10, 0)
            for k in range(8):
                split_lo(G_DOWN + 10, k, last_slot)

            def scale_down(t, nb):
                dve.wait_ge(down_squared, 4 * t + nb + 1)
                return nc.vector.tensor_tensor(y_out[:, t, nb * NB:(nb + 1) * NB], ps[:, 2 * nb + t, :],
                                               gain_ffn[:, nb * NB:(nb + 1) * NB], ALU.mult)

            dve.wait_ge(gain_ffn_landed, 16)
            for t in range(TT):
                for nb in range(3):
                    last = scale_down(t, nb)
                link(last)
                dve.wait_ge(down_squared, 4 * t + 4)
                rms_from_root(down_ss, 2 + t, t, 1)
                for n, (c, n_cols) in enumerate(VECTOR_PIECES[t]):
                    cols = slice(c, c + n_cols)
                    if n == len(VECTOR_PIECES[t]) - 1:
                        link(scale_down(t, 3))
                    nc.vector.scalar_tensor_tensor(out=y_out[:, t, cols], in0=y_out[:, t, cols],
                                                   scalar=out_rms[:, t:t + 1], in1=x2[:, t, cols],
                                                   op0=ALU.mult, op1=ALU.add).then_inc(result, 1)

        @block.tensor
        def _(pe):
            mm = nc.tensor.matmul

            def products(h, k, left, bank, first, last, wait=None, early=None):
                if wait is not None:
                    pe.wait_ge(*wait)
                pe.wait_ge(lo_ready, h + 1)
                hi, lo = w_hi[:, k % HALF_SLOTS, :], w_lo[:, k % HALF_SLOTS, :]
                for t in range(TT):
                    o = ps[:, bank + t, :]
                    for q in range(2):
                        cols = slice(q * NB, (q + 1) * NB)
                        mm(o, left(q, 0, t), hi[:, cols], start=first and q == 0, stop=False,
                           skip_group_check=True)
                        mm(o, left(q, 0, t), lo[:, cols], start=False, stop=False, skip_group_check=True)
                        ins = mm(o, left(q, 1, t), hi[:, cols], start=False, stop=last and q == 1,
                                 skip_group_check=True)
                    if early is not None and t == 0:
                        ins.then_inc(early, 1)
                ins.then_inc(weights_used, 1)

            def from_xt(kt0):
                return lambda q, part, t: xt[:, kt0 + q, part, t * P:(t + 1) * P]

            def fill(f, source):
                pe.wait_ge(fill_lo, f - 3)
                for q in range(2):
                    for t in range(TT):
                        o = ps[:, fill_bank(f), q * SEQ + t * P:q * SEQ + (t + 1) * P]
                        ins = nc.tensor.transpose(o, source(q, t), ident_sb[:])
                ins.then_inc(fill_done, 1)

            def keep_warm(n):
                for _ in range(n):
                    mm(ps[:, 7, 0:P], ones[:], ones[:], start=True, stop=True)

            def first_half():
                left = from_xt(0)
                pe.wait_ge(fill_hi, 1)
                for part, w, ready in ((0, w_hi, (quarter_hi, hi_ready)), (1, w_hi, None),
                                       (0, w_lo, (quarter_lo, lo_ready))):
                    if ready is None:
                        pe.wait_ge(fill_lo, 1)
                    for q in range(2):
                        if ready is not None:
                            pe.wait_ge(ready[q], 1)
                        for t in range(TT):
                            ins = mm(ps[:, t, :], left(q, part, t), w[:, 0, q * NB:(q + 1) * NB],
                                     start=ready is not None and w is w_hi and q == 0, stop=False,
                                     skip_group_check=True)
                ins.then_inc(weights_used, 1)

            pe.wait_ge(ones_ready, 1)
            keep_warm(8)
            first_half()
            for k in range(1, 8):
                products(k, k, from_xt(2 * k), 0, False, k == 7, wait=(fill_lo, k + 1))

            def projection(m, k, bank):
                wait = (z_free, m) if k == 0 else None
                products(8 * m + k, k, from_xt(2 * k), bank, k == 0, k == 7, wait=wait)

            with pe.Fori(0, 5) as i:
                for u in range(2):
                    for k in range(8):
                        projection(2 * i + 1 + u, k, 2 * (1 - u))

            pe.wait_ge(small_landed[1], 16)

            def transposes(s, with_k):
                pe.wait_ge(qk_rotated, s + 1)
                for w in range(2):
                    for t in range(TT):
                        at = w * SEQ + t * P
                        ins = nc.tensor.transpose(ps[:, 4, at:at + P], qk_rot[:, w, t, :], ident_sb[:])
                ins.then_inc(ret_t_done, 1)
                pe.wait_ge(swa_staged, s + 1)
                for w in range(1 + with_k):
                    for t in range(TT):
                        at = w * SEQ + t * P
                        ins = nc.tensor.transpose(ps[:, 5, at:at + P], swa_qk[:, w, t, :], ident_sb[:])
                ins.then_inc(swa_t_done, 1)

            def scores(s):
                pe.wait_ge(ret_t_copied, s + 1)
                mm(ps[:, 6, 0:SEQ], qk_t[:, 1, 0:P], qk_t[:, 0, :], start=True, stop=True)
                mm(ps[:, 6, SEQ:3 * P], qk_t[:, 1, P:SEQ], qk_t[:, 0, P:SEQ], start=True, stop=True)\
                    .then_inc(ret_s_done, 1)
                pe.wait_ge(swa_t_copied, s + 1)
                for a in range(2):
                    rows = slice(64 * a, 64 * a + 64)
                    mm(ps[:, 7 - 2 * a, 0:P], swa_qk_t[rows, 0, 0:P], swa_qk_t[rows, 1, 0:P],
                       start=True, stop=True)
                    ins = mm(ps[:, 7 - 2 * a, P:3 * P], swa_qk_t[rows, 0, P:SEQ], swa_qk_t[rows, 1, :],
                             start=True, stop=True)
                ins.then_inc(swa_s_done, 1)

            def retention_out(s):
                pe.wait_ge(ret_masked, s + 1)
                v = [nat[:, t, bass.ds(RV_AT + RET_DV * s, RET_DV)] for t in range(TT)]
                mm(ps[:, 4, 0:RET_DV], ret_s[:, 0:P], v[0], start=True, stop=True)
                mm(ps[:, 4, RET_DV:], ret_s[:, P:2 * P], v[0], start=True, stop=False)
                mm(ps[:, 4, RET_DV:], ret_s[:, 2 * P:3 * P], v[1], start=False, stop=True)\
                    .then_inc(ret_av_done, 1)

            def window_transposes(s):
                pe.wait_ge(swa_exp, s + 1)
                for a in range(2):
                    for j in range(3):
                        cols = slice(j * P, (j + 1) * P)
                        ins = nc.tensor.transpose(ps[:, 7 - 2 * a, cols], swa_p[:, a, cols], ident_sb[:])
                ins.then_inc(swa_pt_done, 1)

            def window_out(s, kv):
                pe.wait_ge(swa_pt_copied, s + 1)
                v = [nat[:, t, bass.ds(SV_AT + SWA_DH * kv, SWA_DH)] for t in range(TT)]
                for a in range(2):
                    o = [ps[:, 6, SWA_DH * (2 * a + t):SWA_DH * (2 * a + t + 1)] for t in range(TT)]
                    mm(o[0], swa_pt[:, a, 0:P], v[0], start=True, stop=True)
                    mm(o[1], swa_pt[:, a, P:2 * P], v[0], start=True, stop=False)
                    ins = mm(o[1], swa_pt[:, a, 2 * P:3 * P], v[1], start=False, stop=True)
                ins.then_inc(swa_av_done, 1)

            with pe.Fori(0, 4) as i:
                for u in range(2):
                    s = 2 * i + u
                    for k in range(8):
                        if k == 0:
                            transposes(s, u == 0)
                        if k == 1:
                            scores(s)
                        if k == 3:
                            retention_out(s)
                        if k == 4:
                            window_transposes(s)
                        if k == 5:
                            window_out(s, i)
                        projection(2 * i + 11 + u, k, 2 * (1 - u))

            def fill_heads(f):
                at = RV_AT + (f - FILL_RET) * 2 * P if f >= FILL_RET else SQ_AT + (f - FILL_SWA) * 2 * P
                fill(f, lambda q, t: nat[:, t, at + q * P:at + (q + 1) * P])

            pe.wait_ge(swa_out, SWA_HEADS // 2)
            for j in range(4):
                for k in range(8):
                    if k == 0:
                        fill_heads(FILL_SWA + j)
                    projection(19 + j, k, 2 * (1 - j % 2))

            def fill_mix(f):
                at = GR_AT + (f - FILL_MIX) * 2 * P
                pe.wait_ge(mixed_ready, (f - FILL_MIX) // 2 + 1)
                fill(f, lambda q, t: nat[:, t, at + q * P:at + (q + 1) * P])

            pe.wait_ge(ret_gated, 4)
            for n in range(4):
                for k in range(12):
                    if n == 0 and k < 4:
                        fill_heads(FILL_RET + 2 * k)
                        fill_heads(FILL_RET + 2 * k + 1)
                    if n > 0 and k in (2, 3):
                        fill_mix(FILL_MIX + 2 * (n - 1) + k - 2)
                    if k == 0:
                        pe.wait_ge(*((z_free, PROJ_BLOCKS) if n == 0 else (swa_merged, n)))
                    if k == 4:
                        pe.wait_ge(*((z_free, PROJ_BLOCKS + 1) if n == 0 else (mixed_ready, n)))
                    h = H_MERGE + 12 * n + k
                    if k < 4:
                        products(h, k, lambda q, part, t: swa_xt[:, 2 * k + q, part, t * P:(t + 1) * P],
                                 2, k == 0, k == 3, wait=(fill_lo, FILL_SWA + k + 1) if n == 0 else None)
                    else:
                        products(h, k, from_xt(2 * (k - 4)), 0, k == 4, k == 11,
                                 wait=(fill_lo, FILL_RET + k - 4 + 1) if n == 0 else None)

            for p_, banks in enumerate(((2, 4), (0, 2))):
                for k in range(16):
                    group, b, e = k // 4, k // 2 % 2, k % 2
                    kt0 = 4 * group + 2 * e
                    if p_ == 0 and k in (2, 3):
                        fill_mix(FILL_MIX + 6 + k - 2)
                    if k == 0:
                        pe.wait_ge(*((swa_merged, 4) if p_ == 0 else (mixed_ready, 4)))
                    if k == 2:
                        pe.wait_ge(*((fill_lo, FILL_MIX + 6) if p_ == 0 else (out_scaled, TT)))
                    products(H_OUT + 16 * p_ + k, k,
                             lambda q, part, t: mix_view(kt0 + q, 1, part)[:, 0, t * P:(t + 1) * P],
                             banks[b], group == 0 and e == 0, group == 3 and e == 1,
                             wait=(fill_lo, FILL_MIX + kt0 // 2 + 1) if p_ == 0 else None,
                             early=out_tile0 if p_ == 1 and k == 15 else None)

            def up_half(i, k, bank):
                if k == 0 and not (isinstance(i, int) and i == 0):
                    pe.wait_ge(up_free, i)
                pe.wait_ge(lo_ready, 8 * i + (H_UP + k + 1))
                hi, lo = w_hi[:, k % HALF_SLOTS, :], w_lo[:, k % HALF_SLOTS, :]
                kt0 = k % 4 * 4
                for q in range(4):
                    kt = kt0 + q
                    if isinstance(i, int) and i == 0 and k < 4 and q % 2 == 0:
                        pe.wait_ge(fill_lo, FILL_H2 + kt // 2 + 1)
                    for f in range(2):
                        o = ps[:, bank + 2 * (k // 4) + f, :]
                        cols = slice(q * 2 * P + f * P, q * 2 * P + (f + 1) * P)
                        mm(o, hi[:, cols], xt[:, kt, :, :].rearrange("p l t -> p (l t)"),
                           start=kt == 0, stop=False, skip_group_check=True)
                        ins = mm(o[:, 0:SEQ], lo[:, cols], xt[:, kt, 0, :],
                                 start=False, stop=kt == KT - 1, skip_group_check=True)
                ins.then_inc(weights_used, 1)

            def fill_h2(b):
                pe.wait_ge(x2_ready, (2, 4, 6, 6, 6, 6, 7, 7)[b])
                if b >= 4:
                    pe.wait_ge(x2_pool_ready, (2, 3)[b // 2 - 2])
                fill(FILL_H2 + b, lambda q, t: x2[:, t, (2 * b + q) * P:(2 * b + q + 1) * P])

            keep_warm(13)
            for b in range(4):
                fill_h2(b)
            for k in range(8):
                if k in (1, 2):
                    fill_h2(2 * k + 2)
                    fill_h2(2 * k + 3)
                up_half(0, k, 0)
            for k in range(8):
                if k == 2:
                    pe.wait_ge(diag_ready, 1)
                    for n in range(2):
                        for t in range(TT):
                            at = n * SEQ + t * P
                            ins = mm(ps[:, 6, at:at + P], ones[:], diag[:, t, :], start=True, stop=True)
                    ins.then_inc(rms_spread, 1)
                if k == 4:
                    pe.wait_ge(rms_copied, 1)
                up_half(1, k, 4)
            with pe.Fori(0, 10) as ii:
                for u in range(2):
                    for k in range(8):
                        up_half(2 * ii + 2 + u, k, 4 * u)

            def down(i, par, first):
                for k in range(8):
                    if k == 0:
                        pe.wait_ge(y_lo, i + 1)
                    if first and k in (0, 4):
                        pe.wait_ge(up_free, UP_GROUPS + k // 4)
                    e = k % 2
                    products(8 * i + (H_DOWN + k), k,
                             lambda q, part, t: y_split[:, par, 2 * e + q, part, t * P:(t + 1) * P],
                             2 * (k // 2), first and e == 0, False)

            def down_last(par):
                pe.wait_ge(y_lo, DOWN_GROUPS)
                for t in range(TT):
                    for k in range(8):
                        if t == 0:
                            pe.wait_ge(lo_ready, H_DOWN + 8 * (DOWN_GROUPS - 1) + k + 1)
                        hi, lo = last_slot(k, 0), last_slot(k, 1)
                        o = ps[:, 2 * (k // 2) + t, :]
                        for q in range(2):
                            cols = slice(q * NB, (q + 1) * NB)
                            yh, yl = (y_split[:, par, 2 * (k % 2) + q, part, t * P:(t + 1) * P]
                                      for part in range(2))
                            mm(o, yh, hi[:, cols], start=False, stop=False, skip_group_check=True)
                            mm(o, yh, lo[:, cols], start=False, stop=False, skip_group_check=True)
                            ins = mm(o, yl, hi[:, cols], start=False, stop=k % 2 == 1 and q == 1,
                                     skip_group_check=True)
                        ins.then_inc(last_used, 1)

            down(0, 0, True)
            with pe.Fori(0, 4) as ii:
                for u in range(2):
                    down(2 * ii + 1 + u, 1 - u, False)
            down(9, 1, False)
            down_last(0)


def _tables():
    pos = np.arange(SEQ, dtype=np.float32)
    inv = (1.0 / (np.float32(10000.0) ** (np.arange(0, RET_DK, 2, dtype=np.float32) / RET_DK))).astype(np.float32)
    ang = (pos[:, None] * inv[None, :]).astype(np.float32)
    cs = np.stack([np.cos(ang), np.sin(ang)])
    cs = cs.reshape(2, TT, P, 64).transpose(2, 0, 1, 3)
    rope = np.ascontiguousarray(np.broadcast_to(cs[:, :, None], (P, 2, 2, TT, 64))).astype(np.float32)
    log_gamma = np.log(1.0 - 2.0 ** (-5.0 - np.arange(RET_HEADS, dtype=np.float64)))
    rel = np.arange(2 * P)[None, :] - np.arange(P)[:, None]
    decay = np.where(rel[:, None] >= 0, np.exp(log_gamma[None, :, None] * np.maximum(rel, 0)[:, None]), 0.0)
    decay = (decay * RET_DK ** -0.5).astype(np.float32)
    q, k = np.arange(P)[:, None], np.arange(P)[None, :]
    same = np.where(k <= q, 0.0, MASKED)
    before = np.where(k > q, 0.0, MASKED)
    band = np.concatenate([same, before, same], axis=1).astype(np.float32)
    return np.eye(P, dtype=np.float32), decay, rope, band


def _weight_stream(w_in, w_ret_o, w_swa_o, w_out, w_up, w_down):
    def blocks(w):
        k, n = w.shape
        return w.reshape(k // (4 * P), 4, P, n // NB, NB).transpose(3, 0, 2, 1, 4)

    order = [14, 0, 1, 2, 3, 4, 5, 6, 7, 12, 13, 8, 9, 10, 11, 15, 16, 17, 18, 19, 20, 21, 22]
    parts = [blocks(w_in)[order]]
    parts.append(np.concatenate([blocks(w_swa_o), blocks(w_ret_o)], axis=1))
    o = blocks(w_out)
    parts.append(o.reshape(2, 2, *o.shape[1:]).transpose(0, 2, 1, 3, 4, 5))
    up = w_up.reshape(2, 8, P, 2, UP_GROUPS, 256)
    parts.append(up.transpose(4, 3, 0, 2, 1, 5))
    down = w_down.reshape(DOWN_GROUPS, 4, P, 4, NB)
    parts.append(down.transpose(0, 3, 2, 1, 4))
    return np.concatenate([a.reshape(-1, P, CHUNK) for a in parts], axis=0)


def kernel(x, g_pre_mix, w_in, w_ret_o, w_swa_o, w_out, swa_sinks, g_post_mix,
           g_pre_ffn, w_up, conv_w, conv_b, w_down, g_post_ffn):
    import concourse.bacc as bacc
    from concourse.bass_utils import run_bass_kernel_spmd

    a = {k: np.asarray(v) for k, v in locals().items() if k not in ("bacc", "run_bass_kernel_spmd")}
    ident, decay, rope, band = _tables()
    arrays = {
        "weights": _weight_stream(a["w_in"][0], a["w_ret_o"][0], a["w_swa_o"][0], a["w_out"][0],
                                  a["w_up"][0], a["w_down"][0]),
        "x": a["x"][0],
        "x_t": np.ascontiguousarray(a["x"][0].T.reshape(KT, P, SEQ).transpose(1, 0, 2)),
        "g_pre": np.ascontiguousarray(a["g_pre_mix"][0].reshape(KT, P).T),
        "g_ffn": np.ascontiguousarray(a["g_pre_ffn"][0].reshape(KT, P).T),
        "g_post_mix": np.ascontiguousarray(np.broadcast_to(a["g_post_mix"][0], (P, D_MODEL))),
        "g_post_ffn": np.ascontiguousarray(np.broadcast_to(a["g_post_ffn"][0], (P, D_MODEL))),
        "sinks": np.ascontiguousarray(np.broadcast_to(np.repeat(a["swa_sinks"][0], TT), (P, TT * SWA_HEADS))),
        "conv": np.ascontiguousarray(np.concatenate([a["conv_w"][0], a["conv_b"]], axis=0)
                                     .reshape(4, 2 * FF_TILES, P).transpose(2, 1, 0)),
        "ident": ident, "decay": decay, "rope": rope, "band": band,
    }
    nc = bacc.Bacc("TRN2", target_bir_lowering=False, num_devices=1)
    args = {k: nc.dram_tensor(k, v.shape, mybir.dt.from_np(v.dtype), kind="ExternalInput").ap()
            for k, v in arrays.items()}
    out = nc.dram_tensor("out", (SEQ, D_MODEL), F32, kind="ExternalOutput").ap()
    build(nc, out=out, **args)
    r = run_bass_kernel_spmd(nc, [arrays], core_ids=[0])
    return r.results[0]["out"].reshape(1, SEQ, D_MODEL)
```
